# Optimizing a Trainium2 kernel written in Bass

```python
import math
import jax, jax.numpy as jnp
from jax import lax
import numpy as np

D_MODEL = 1024
BATCH = 1
SEQ = 512
DEPTH = 1

NSA_HEADS = 16
NSA_KV_GROUPS = 4
NSA_Q_PER_GROUP = NSA_HEADS // NSA_KV_GROUPS
NSA_HEAD_DIM = 64
CMP_BLOCK = 32
CMP_STRIDE = 16
CMP_HIDDEN = 4 * NSA_HEAD_DIM
SEL_BLOCK = 64
SEL_TOPK = 8
WINDOW = 512
Q_BLOCK = 64
SSM_D_INNER = 2 * D_MODEL
SSM_HEAD_DIM = 64
SSM_HEADS = SSM_D_INNER // SSM_HEAD_DIM
SSM_GROUPS = 4
SSM_STATE = 128
SSM_CONV = 4
SSM_CHUNK = 128
FFN_HIDDEN = 2816
FFN_CONV = 3
Q_W = NSA_HEADS * NSA_HEAD_DIM
KV_W = NSA_KV_GROUPS * NSA_HEAD_DIM
NSA_GATE_W = 3 * NSA_HEADS
SSM_BC_W = SSM_GROUPS * SSM_STATE
SSM_XBC_W = SSM_D_INNER + 2 * SSM_BC_W
IN_SIZES = (Q_W, KV_W, KV_W, KV_W, KV_W, KV_W, KV_W, NSA_GATE_W, SSM_D_INNER, SSM_XBC_W, SSM_HEADS, D_MODEL, D_MODEL)
IN_W = Q_W + 6 * KV_W + NSA_GATE_W + SSM_D_INNER + SSM_XBC_W + SSM_HEADS + 2 * D_MODEL
EPS = 1e-6
NEG_INF = -1e30

kernel_name = 'hybrid_nsa_ssd_convglu_block'

def rms_norm(x, w):
    xf = x.astype(jnp.float32)
    y = xf * lax.rsqrt(jnp.mean(xf * xf, axis=-1, keepdims=True) + EPS)
    return (y * w.astype(jnp.float32)).astype(x.dtype)

def causal_depthwise_conv(x, w, b):
    width = w.shape[0]
    y = lax.conv_general_dilated(x, w[:, None, :].astype(x.dtype), window_strides=(1,),
                                 padding=[(width - 1, 0)], dimension_numbers=('NWC', 'WIO', 'NWC'),
                                 feature_group_count=x.shape[-1])
    return y + b.astype(x.dtype)

def split_columns(u, sizes):
    return jnp.split(u, np.cumsum(sizes)[:-1].tolist(), axis=-1)

def alibi_slopes():
    h = jnp.arange(1, NSA_HEADS + 1, dtype=jnp.float32)
    return jnp.exp2(-8.0 * h / NSA_HEADS).reshape(NSA_KV_GROUPS, NSA_Q_PER_GROUP)

def masked_softmax(s, mask):
    return jax.nn.softmax(jnp.where(mask, s, NEG_INF), axis=-1)

def compress_blocks(kv, tok_idx, pe, w1, w2):
    blk = kv[:, tok_idx] + pe[None, None, :, None, :].astype(kv.dtype)
    b, nc = blk.shape[:2]
    flat = jnp.transpose(blk, (0, 1, 3, 2, 4)).reshape(b, nc, NSA_KV_GROUPS, CMP_BLOCK * NSA_HEAD_DIM)
    return jax.nn.silu(flat @ w1) @ w2

def nsa_mixer(q, k_cmp, v_cmp, k_sel, v_sel, k_win, v_win, g_branch,
              q_gain, k_gain, pe_k, pe_v, wk1, wk2, wv1, wv2):
    b, s = q.shape[:2]
    G, R, dh = NSA_KV_GROUPS, NSA_Q_PER_GROUP, NSA_HEAD_DIM
    f32 = jnp.float32
    q = rms_norm(q.reshape(b, s, G, R, dh), q_gain) * (dh ** -0.5)
    q = jnp.transpose(q, (0, 2, 3, 1, 4))

    def kv_heads(u):
        return u.reshape(b, s, G, dh)

    nc = (s - CMP_BLOCK) // CMP_STRIDE + 1
    cmp_start = jnp.arange(nc) * CMP_STRIDE
    tok_idx = cmp_start[:, None] + jnp.arange(CMP_BLOCK)[None, :]
    cmp_end = cmp_start + CMP_BLOCK - 1
    kc = rms_norm(compress_blocks(kv_heads(k_cmp), tok_idx, pe_k, wk1, wk2), k_gain[0]).transpose(0, 2, 1, 3)
    vc = compress_blocks(kv_heads(v_cmp), tok_idx, pe_v, wv1, wv2).transpose(0, 2, 1, 3)

    nb = s // SEL_BLOCK
    n_sel = min(SEL_TOPK, nb)
    ks = rms_norm(kv_heads(k_sel), k_gain[1]).transpose(0, 2, 1, 3).reshape(b, G, nb, SEL_BLOCK, dh)
    vs = kv_heads(v_sel).transpose(0, 2, 1, 3).reshape(b, G, nb, SEL_BLOCK, dh)
    blk_start = jnp.arange(nb) * SEL_BLOCK
    overlap = ((cmp_start[:, None] <= blk_start[None, :] + SEL_BLOCK - 1)
               & (cmp_end[:, None] >= blk_start[None, :])).astype(f32)

    pad = ((0, 0), (0, 0), (WINDOW, 0), (0, 0))
    kw = jnp.pad(rms_norm(kv_heads(k_win), k_gain[2]).transpose(0, 2, 1, 3), pad)
    vw = jnp.pad(kv_heads(v_win).transpose(0, 2, 1, 3), pad)

    slopes = alibi_slopes()[None, :, :, None, None]
    nqb = s // Q_BLOCK
    q_blocks = jnp.moveaxis(q.reshape(b, G, R, nqb, Q_BLOCK, dh), 3, 0)
    gates = jax.nn.sigmoid(g_branch.astype(f32)).reshape(b, nqb, Q_BLOCK, G, R, 3)
    g_blocks = jnp.transpose(gates, (1, 0, 3, 4, 2, 5))
    bi = jnp.arange(b)[:, None, None, None]
    gi = jnp.arange(G)[None, :, None, None]

    def attend_block(args):
        qb, gb, i = args
        start = i * Q_BLOCK
        t = start + jnp.arange(Q_BLOCK)
        s_c = jnp.einsum('bgrqd,bgcd->bgrqc', qb, kc).astype(f32)
        d_c = t[:, None] - cmp_end[None, :]
        vis_c = d_c >= 0
        p_c = masked_softmax(s_c - slopes * d_c, vis_c) * jnp.any(vis_c, axis=-1, keepdims=True)
        o_c = jnp.einsum('bgrqc,bgcd->bgrqd', p_c.astype(vc.dtype), vc)
        imp = jnp.einsum('bgrqc,cj->bgqj', p_c, overlap)
        cur = t // SEL_BLOCK
        j = jnp.arange(nb)[None, :]
        forced = (j == 0) | (j == cur[:, None]) | (j == cur[:, None] - 1)
        causal_blk = j * SEL_BLOCK <= t[:, None]
        score = jnp.where(forced, jnp.inf, jnp.where(causal_blk, imp, -jnp.inf))
        _, idx = lax.top_k(score, n_sel)
        k_g = ks[bi, gi, idx].reshape(b, G, Q_BLOCK, n_sel * SEL_BLOCK, dh)
        v_g = vs[bi, gi, idx].reshape(b, G, Q_BLOCK, n_sel * SEL_BLOCK, dh)
        pos = (idx[..., None] * SEL_BLOCK + jnp.arange(SEL_BLOCK)).reshape(b, G, Q_BLOCK, n_sel * SEL_BLOCK)
        d_s = (t[:, None] - pos)[:, :, None]
        s_s = jnp.einsum('bgrqd,bgqkd->bgrqk', qb, k_g).astype(f32)
        p_s = masked_softmax(s_s - slopes * d_s, d_s >= 0)
        o_s = jnp.einsum('bgrqk,bgqkd->bgrqd', p_s.astype(v_g.dtype), v_g)
        k_w = lax.dynamic_slice_in_dim(kw, start, Q_BLOCK + WINDOW, axis=2)
        v_w = lax.dynamic_slice_in_dim(vw, start, Q_BLOCK + WINDOW, axis=2)
        pos_w = start - WINDOW + jnp.arange(Q_BLOCK + WINDOW)
        d_w = t[:, None] - pos_w[None, :]
        vis_w = (d_w >= 0) & (d_w < WINDOW) & (pos_w[None, :] >= 0)
        s_w = jnp.einsum('bgrqd,bgkd->bgrqk', qb, k_w).astype(f32)
        p_w = masked_softmax(s_w - slopes * d_w, vis_w)
        o_w = jnp.einsum('bgrqk,bgkd->bgrqd', p_w.astype(v_w.dtype), v_w)
        return gb[..., 0:1] * o_c + gb[..., 1:2] * o_s + gb[..., 2:3] * o_w

    o = lax.map(attend_block, (q_blocks, g_blocks, jnp.arange(nqb)))
    return jnp.transpose(o, (1, 0, 4, 2, 3, 5)).reshape(b, s, NSA_HEADS * dh).astype(v_cmp.dtype)

def segsum(a):
    n = a.shape[-1]
    a_rep = jnp.broadcast_to(a[..., :, None], a.shape + (n,))
    a_rep = jnp.where(jnp.tril(jnp.ones((n, n), bool), -1), a_rep, 0.0)
    seg = jnp.cumsum(a_rep, axis=-2)
    return jnp.where(jnp.tril(jnp.ones((n, n), bool), 0), seg, -jnp.inf)

def ssd_chunked(x, dt, a, bm, cm):
    b, s = x.shape[:2]
    nc, L, G, E = s // SSM_CHUNK, SSM_CHUNK, SSM_GROUPS, SSM_HEADS // SSM_GROUPS
    f32 = jnp.float32
    x = x.reshape(b, nc, L, G, E, SSM_HEAD_DIM).astype(f32)
    dt = dt.reshape(b, nc, L, G, E)
    xdt = x * dt[..., None]
    a_dt = jnp.transpose(dt * a.reshape(G, E), (0, 3, 4, 1, 2))
    bm = bm.reshape(b, nc, L, G, SSM_STATE).astype(f32)
    cm = cm.reshape(b, nc, L, G, SSM_STATE).astype(f32)
    a_cum = jnp.cumsum(a_dt, axis=-1)
    decay_mat = jnp.exp(segsum(a_dt))
    cb = jnp.einsum('bclgn,bcsgn->bgcls', cm, bm)
    y_diag = jnp.einsum('bgecls,bcsgep->bclgep', cb[:, :, None] * decay_mat, xdt)
    decay_states = jnp.exp(a_cum[..., -1:] - a_cum)
    states = jnp.einsum('bclgn,bgecl,bclgep->bcgepn', bm, decay_states, xdt)
    chunk_decay = jnp.exp(a_cum[..., -1])

    def step(h, inp):
        st, dec = inp
        return dec[..., None, None] * h + st, h

    h0 = jnp.zeros((b, G, E, SSM_HEAD_DIM, SSM_STATE), f32)
    _, prev = lax.scan(step, h0, (jnp.moveaxis(states, 1, 0), jnp.moveaxis(chunk_decay, 3, 0)))
    prev = jnp.moveaxis(prev, 0, 1)
    y_off = jnp.einsum('bclgn,bcgepn,bgecl->bclgep', cm, prev, jnp.exp(a_cum))
    return (y_diag + y_off).reshape(b, s, SSM_HEADS, SSM_HEAD_DIM)

def ssd_mixer(z, xbc, dt_raw, conv_w, conv_b, dt_bias, a_log, d_skip, norm_w):
    b, s = z.shape[:2]
    f32 = jnp.float32
    xbc = jax.nn.silu(causal_depthwise_conv(xbc, conv_w, conv_b))
    xs, bm, cm = split_columns(xbc, (SSM_D_INNER, SSM_BC_W, SSM_BC_W))
    xs = xs.reshape(b, s, SSM_HEADS, SSM_HEAD_DIM)
    bm = bm.reshape(b, s, SSM_GROUPS, SSM_STATE)
    cm = cm.reshape(b, s, SSM_GROUPS, SSM_STATE)
    dt = jax.nn.softplus(dt_raw.astype(f32) + dt_bias.astype(f32))
    a = -jnp.exp(a_log.astype(f32))
    y = ssd_chunked(xs, dt, a, bm, cm) + d_skip.astype(f32)[:, None] * xs.astype(f32)
    y = y.reshape(b, s, SSM_D_INNER) * jax.nn.silu(z.astype(f32))
    yg = y.reshape(b, s, SSM_GROUPS, SSM_D_INNER // SSM_GROUPS)
    yg = yg * lax.rsqrt(jnp.mean(yg * yg, axis=-1, keepdims=True) + EPS)
    return (yg.reshape(b, s, SSM_D_INNER) * norm_w.astype(f32)).astype(z.dtype)

def conv_glu_ffn(h, w_up, conv_w, conv_b, w_down):
    u = causal_depthwise_conv(h @ w_up, conv_w, conv_b)
    gate, val = jnp.split(u, 2, axis=-1)
    return (jax.nn.silu(gate) * val) @ w_down

def setup_inputs(seed: int = 0) -> dict:
    key = jax.random.key(seed)
    k = jax.random.split(key, 32)
    f32 = jnp.float32
    L = DEPTH
    dh = NSA_HEAD_DIM

    def nrm(kk, shape, scale):
        return jax.random.normal(kk, shape, f32) * scale

    dt0 = jnp.exp(jax.random.uniform(k[14], (L, SSM_HEADS), f32, math.log(1e-3), math.log(1e-1)))
    return {
        'x': nrm(k[0], (BATCH, SEQ, D_MODEL), 1.0),
        'norm1_w': 1.0 + nrm(k[1], (L, D_MODEL), 0.02),
        'w_in': nrm(k[2], (L, D_MODEL, IN_W), D_MODEL ** -0.5),
        'nsa_q_gain': 1.0 + nrm(k[3], (L, dh), 0.02),
        'nsa_k_gain': 1.0 + nrm(k[4], (L, 3, dh), 0.02),
        'cmp_pe_k': nrm(k[5], (L, CMP_BLOCK, dh), 0.02),
        'cmp_pe_v': nrm(k[6], (L, CMP_BLOCK, dh), 0.02),
        'cmp_wk1': nrm(k[7], (L, CMP_BLOCK * dh, CMP_HIDDEN), (CMP_BLOCK * dh) ** -0.5),
        'cmp_wk2': nrm(k[8], (L, CMP_HIDDEN, dh), CMP_HIDDEN ** -0.5),
        'cmp_wv1': nrm(k[9], (L, CMP_BLOCK * dh, CMP_HIDDEN), (CMP_BLOCK * dh) ** -0.5),
        'cmp_wv2': nrm(k[10], (L, CMP_HIDDEN, dh), CMP_HIDDEN ** -0.5),
        'ssm_conv_w': nrm(k[11], (L, SSM_CONV, SSM_XBC_W), SSM_CONV ** -0.5),
        'ssm_conv_b': nrm(k[12], (L, SSM_XBC_W), 0.01),
        'ssm_dt_bias': dt0 + jnp.log(-jnp.expm1(-dt0)),
        'ssm_a_log': jnp.log(jax.random.uniform(k[13], (L, SSM_HEADS), f32, 1.0, 16.0)),
        'ssm_d': 1.0 + nrm(k[15], (L, SSM_HEADS), 0.01),
        'ssm_norm_w': 1.0 + nrm(k[16], (L, SSM_D_INNER), 0.02),
        'w_proj_a': nrm(k[17], (L, Q_W, D_MODEL), Q_W ** -0.5),
        'w_proj_b': nrm(k[18], (L, SSM_D_INNER, D_MODEL), SSM_D_INNER ** -0.5),
        'w_out': nrm(k[19], (L, D_MODEL, D_MODEL), D_MODEL ** -0.5),
        'norm2_w': 1.0 + nrm(k[20], (L, D_MODEL), 0.02),
        'ffn_w_up': nrm(k[21], (L, D_MODEL, 2 * FFN_HIDDEN), D_MODEL ** -0.5),
        'ffn_conv_w': nrm(k[22], (L, FFN_CONV, 2 * FFN_HIDDEN), FFN_CONV ** -0.5),
        'ffn_conv_b': nrm(k[23], (L, 2 * FFN_HIDDEN), 0.01),
        'ffn_w_down': nrm(k[24], (L, FFN_HIDDEN, D_MODEL), FFN_HIDDEN ** -0.5),
    }

def reference(x, norm1_w, w_in, nsa_q_gain, nsa_k_gain, cmp_pe_k, cmp_pe_v, cmp_wk1, cmp_wk2,
              cmp_wv1, cmp_wv2, ssm_conv_w, ssm_conv_b, ssm_dt_bias, ssm_a_log, ssm_d, ssm_norm_w,
              w_proj_a, w_proj_b, w_out, norm2_w, ffn_w_up, ffn_conv_w, ffn_conv_b, ffn_w_down):
    for layer in range(DEPTH):
        h = rms_norm(x, norm1_w[layer])
        (q, k_c, v_c, k_s, v_s, k_w, v_w, g_nsa, z, xbc, dt_raw,
         gate_a, gate_b) = split_columns(h @ w_in[layer], IN_SIZES)
        y_a = nsa_mixer(q, k_c, v_c, k_s, v_s, k_w, v_w, g_nsa, nsa_q_gain[layer], nsa_k_gain[layer],
                        cmp_pe_k[layer], cmp_pe_v[layer], cmp_wk1[layer], cmp_wk2[layer],
                        cmp_wv1[layer], cmp_wv2[layer])
        y_b = ssd_mixer(z, xbc, dt_raw, ssm_conv_w[layer], ssm_conv_b[layer], ssm_dt_bias[layer],
                        ssm_a_log[layer], ssm_d[layer], ssm_norm_w[layer])
        merged = jax.nn.sigmoid(gate_a) * (y_a @ w_proj_a[layer]) + jax.nn.sigmoid(gate_b) * (y_b @ w_proj_b[layer])
        x = x + merged @ w_out[layer]
        x = x + conv_glu_ffn(rms_norm(x, norm2_w[layer]), ffn_w_up[layer], ffn_conv_w[layer],
                             ffn_conv_b[layer], ffn_w_down[layer])
    return x


_drawn_inputs = setup_inputs


def setup_inputs(seed=0):
    import zlib

    import numpy as np

    out = dict(_drawn_inputs(seed))
    spreads = {}
    factors = {'norm1_w': 3.089,
     'nsa_q_gain': 8.0,
     'nsa_k_gain': 8.0,
     'cmp_pe_k': 8.0,
     'cmp_pe_v': 31.114,
     'ssm_conv_b': 7.769,
     'ssm_d': 64.0,
     'ssm_norm_w': 5.524,
     'norm2_w': 4.363,
     'ffn_conv_b': 8.0}
    for name, (base, spread) in spreads.items():
        noise = np.random.default_rng([zlib.crc32(name.encode()), seed]).standard_normal(out[name].shape)
        drawn = base * np.exp(spread * noise) if base else spread * noise
        out[name] = __import__('jax').numpy.asarray(drawn.astype(out[name].dtype))
    for name, factor in factors.items():
        out[name] = (out[name] * factor).astype(out[name].dtype)
    return out
```

```python
from contextlib import ExitStack

import concourse.bass as bass
from concourse import mybir

F32 = mybir.dt.float32
F32R = mybir.dt.float32r
I32 = mybir.dt.int32
ALU = mybir.AluOpType
ACT = mybir.ActivationFunctionType
AX = mybir.AxisListType
ds = bass.ds

P = 128
T = 512
NT = T // P
D = 1024
KD = D // P
G = 4
R = 4
DH = 64
NH = G * R
NC = (T - 32) // 16 + 1
SH = 32
SE = SH // G
SD = 2048
F = 2816
FB = F // P
EPS = 1e-6
NEG = -1e30

C_Q, C_KC, C_VC, C_KS, C_VS, C_KW, C_VW = 0, 1024, 1280, 1536, 1792, 2048, 2304
C_GATE, C_Z, C_X = 2560, 2608, 4656
C_B, C_C = C_X + SD, C_X + SD + 512
C_DT, C_GA, C_GB = 7728, 7760, 8784

CW, CB_, QG, KG = 0, 96, 120, 121
FW01, PEK, PEV = 0, 88, 104
FW2, FBI, N1, N2, SN = 0, 44, 88, 96, 104

PRE_BLOCKS = 5
GROUP_BLOCKS = 14
U_GRP = B_GRP = PRE_BLOCKS
U_MRG = B_MRG = PRE_BLOCKS + G * GROUP_BLOCKS
U_OUT, B_OUT = U_MRG + 5 * KD, B_MRG + 4 * KD
U_UP, B_UP = U_OUT + KD, B_OUT + KD
U_DN, B_DN = U_UP + 2 * FB, B_UP + 2 * FB
UNITS = U_DN + 3 * KD
BQA, BQB, BKS, BKW, BX, BB, BC, BZ = 0, 1, 2, 3, 4, 8, 9, 10

ACT_GRP = 2
DVE_GRP = 138


class Count:

    def __init__(self, eng, sem):
        self.eng, self.sem, self.base, self.k, self.i, self.per = eng, sem, 0, 0, None, 0

    def value(self):
        return self.base + self.k if self.i is None else self.i * self.per + (self.base + self.k)

    def done(self, ins):
        ins.then_inc(self.sem, 1)
        self.k += 1

    def fence(self):
        self.eng.wait_ge(self.sem, self.value())

    def loop(self, i, per):
        self.base, self.k, self.i, self.per = self.base + self.k, 0, i, per

    def end(self, trips):
        assert self.k == self.per, (self.k, self.per)
        self.base, self.k, self.i = self.base + trips * self.per, 0, None


def wait_alone(eng, sem, value, passed):
    eng.wait_ge(sem, value)
    eng.sem_inc(passed, 1)


def program(nc, io, out, spill):
    with ExitStack() as ctx:
        def sb(name, shape, dt=F32, c=ctx):
            return c.enter_context(nc.sbuf_tensor(name, shape, dt))

        def bank(name):
            return ctx.enter_context(nc.psum_tensor(name, [P, 512], F32))

        def sem(name):
            return ctx.enter_context(nc.semaphore(name))

        wraw = [sb(f"wraw{s}", [P, 8, P]) for s in range(2)]
        whi = [sb(f"whi{s}", [P, 8, P], F32R) for s in range(2)]
        wlo = [sb(f"wlo{s}", [P, 8, P], F32R) for s in range(2)]
        ident = sb("ident", [P, P])
        pcol = sb("pcol", [P, 3, P])
        stat = sb("stat", [P, NT])
        rstd = sb("rstd", [P, 32])
        newton = [sb(f"newton{i}", [P, 32]) for i in range(4)]
        hstage = [sb(f"hstage{i}", [P, T]) for i in range(2)]

        ph12 = ExitStack()
        hT = [sb("hT_hi", [P, KD, T], F32R, ph12), sb("hT_lo", [P, KD, T], F32R, ph12)]
        ph1 = ExitStack()
        tri_le = sb("tri_le", [P, P], c=ph1)
        gt = sb("strict_gt", [P, P], c=ph1)
        ones = sb("ones", [P, P], c=ph1)
        negdist = sb("negdist", [P, T], c=ph1)
        cmask = sb("cmask", [P, T], c=ph1)
        negdist_c = sb("negdist_c", [P, NT, NC], c=ph1)
        cmask_c = sb("cmask_c", [P, NT, NC], c=ph1)
        anyvis = sb("anyvis", [P, NT], c=ph1)
        slopes = sb("slopes", [P, NH], c=ph1)
        gates = sb("gates", [P, NT, 48], c=ph1)
        dt_all = sb("dt_all", [P, NT, SH], c=ph1)
        adt = sb("adt", [P, NT, SH], c=ph1)
        dec = sb("dec", [P, 3, NT, SH], c=ph1)
        drow = sb("drow", [P, 3, SH], c=ph1)
        kcT = sb("kcT", [P, G, 32], c=ph1)
        vc_all = sb("vc_all", [NC, G, DH], c=ph1)

        pre = ExitStack()
        xt = sb("xt", [P, NT, D], c=pre)
        prow = sb("prow", [P, 3, P], c=pre)
        small = sb("small", [P, T], c=pre)
        spt = [sb(f"spt{i}", [P, NT, SH], c=pre) for i in range(6)]
        sqj = sb("sqj", [P, D], c=pre)
        cst = [sb(f"cst{i}", [P, G, T], c=pre) for i in range(2)]
        cw1 = [sb(f"cw1_{i}", [P, 16, 256], c=pre) for i in range(2)]
        cw2 = [sb(f"cw2_{i}", [P, 2, DH], c=pre) for i in range(2)]
        pebias = sb("pebias", [P, 4], c=pre)
        hid = sb("hid", [P, 4, G * NC], c=pre)
        kv_c = sb("kv_c", [NC, 2, G, DH], c=pre)
        sq_c = sb("sq_c", [NC, G, DH], c=pre)
        kdup = sb("kdup", [NC, G, 2, DH], c=pre)
        pre.close()

        chan = [sb(f"chan{i}", [P, T], c=ph1) for i in range(2)]
        tok = sb("tok", [P, 4, NT, P], c=ph1)
        sq = sb("sq", [P, NT, P], c=ph1)
        ss = sb("ss", [P, 4, 8], c=ph1)
        tokn = [sb(f"tokn{i}", [P, NT, P], c=ph1) for i in range(2)]
        qT = [sb(f"qT{i}", [P, T], c=ph1) for i in range(2)]
        kT = [sb(f"kT{i}", [P, T], c=ph1) for i in range(2)]
        kcg = sb("kcg", [P, NC], c=ph1)
        vcg = sb("vcg", [NC, DH], c=ph1)
        hbias = [sb(f"hbias{i}", [P, T], c=ph1) for i in range(2)]
        cbias = sb("cbias", [P, NT, R, NC], c=ph1)
        cs = sb("cs", [P, NT, R, NC], c=ph1)
        cstat = sb("cstat", [P, 3, NT * R], c=ph1)
        WID = 1280
        off = {3: 0, 2: 512, 1: 896, 0: 1152}
        negmx = [sb(f"negmx{i}", [P, NT], c=ph1) for i in range(2)]
        rsum = [sb(f"rsum{i}", [P, NT], c=ph1) for i in range(2)]
        pscale = [sb(f"pscale{i}", [P, NT], c=ph1) for i in range(2)]
        pT = sb("pT", [P, WID], c=ph1)
        offT = [0, 512, 896, 1152]
        ycopy = sb("ycopy", [P, T], c=ph1)
        ysp = [[sb(f"y{h}{i}", [P, T], F32R, ph1) for h in ("hi", "lo")] for i in range(2)]
        xraw = [sb(f"xraw{i}", [P, T], c=ph1) for i in range(2)]
        xc = sb("xc", [P, 6, T], c=ph1)
        zchan = sb("zchan", [P, 4, T], c=ph1)
        amask = [sb(f"amask{i}", [P, 4, P], c=ph1) for i in range(2)]
        Ldec = [sb(f"Ldec{i}", [P, 4, P], c=ph1) for i in range(2)]
        state = sb("state", [P, 3, T], c=ph1)
        stc = sb("stc", [P, 2, T], c=ph1)
        yoff = sb("yoff", [P, 3, T], c=ph1)

        piece_a = sb("piece_a", [P, 2 * WID], c=ph1)
        piece_b = sb("piece_b", [P, 2 * WID], c=ph1)
        piece_c = sb("piece_c", [P, R * T], c=ph1)
        sneg = [piece_a[:, WID * i:WID * (i + 1)] for i in range(2)]
        prob = [piece_b[:, WID * i:WID * (i + 1)] for i in range(2)]
        pcT = piece_c[0:NC, :].rearrange("p (r t) -> p r t", r=R)
        xdt = piece_a[:, 0:NT * T].rearrange("p (c t) -> p c t", c=NT)
        xdt2 = piece_b[:, 0:3 * T].rearrange("p (c t) -> p c t", c=3)
        Bt = piece_b[:, 3 * T:4 * T].rearrange("p (c n) -> p c n", c=NT)
        CBm = piece_b[:, 4 * T:5 * T].rearrange("p (c n) -> p c n", c=NT)
        zs = piece_c[:, :].rearrange("p (c t) -> p c t", c=NT)
        Xt = tok[:, :, :, :].rearrange("p c a n -> p c (a n)")
        ph1.close()

        ph2 = ExitStack()
        yT = [sb("yT_hi", [P, 24, T], F32R, ph2), sb("yT_lo", [P, 24, T], F32R, ph2)]
        mT = [sb("mT_hi", [P, KD, T], F32R, ph2), sb("mT_lo", [P, KD, T], F32R, ph2)]
        sg = sb("sg", [P, 2, T], c=ph2)
        pj = sb("pj", [P, 2, T], c=ph2)
        ph2.close()
        ph12.close()

        ph3 = ExitStack()
        x1 = sb("x1", [P, NT, D], c=ph3)
        xres = sb("xres", [P, NT, D], c=ph3)
        ochan = [sb(f"ochan{i}", [P, T], c=ph3) for i in range(2)]
        otok = [sb(f"otok{i}", [P, NT, P], c=ph3) for i in range(2)]
        otile = [sb(f"otile{i}", [P, NT, P], c=ph3) for i in range(2)]
        u_rw = sb("u_raw", [P, 2 * T], c=ph3)
        u_raw = [u_rw[:, T * i:T * (i + 1)] for i in range(2)]
        u_c = [sb(f"u_c{i}", [P, T], c=ph3) for i in range(2)]
        u_a = sb("u_a", [P, T], c=ph3)
        h2T = [sb("h2T_hi", [P, KD, T], F32R, ph3), sb("h2T_lo", [P, KD, T], F32R, ph3)]
        aT = [sb("aT_hi", [P, FB, T], F32R, ph3), sb("aT_lo", [P, FB, T], F32R, ph3)]
        ph3.close()

        gb = [bank("g0"), bank("g1")]
        tb = [bank("t0"), bank("t1")]
        s0, s1, s2, ob = bank("s0"), bank("s1"), bank("s2"), bank("ob")

        w_loaded = [sem("w_loaded0"), sem("w_loaded1")]
        w_hi, w_lo, mm_done, g_rel = sem("w_hi"), sem("w_lo"), sem("mm_done"), sem("g_rel")
        x_loaded, p_loaded, c_loaded = sem("x_loaded"), sem("p_loaded"), sem("c_loaded")
        sp_passed, dve_passed = sem("sp_passed"), sem("dve_passed")
        const_ready, prow_zero = sem("const_ready"), sem("prow_zero")
        t_fill, t_rel = sem("t_fill"), sem("t_rel")
        act_seq, dve_seq, pool_seq = sem("act_seq"), sem("dve_seq"), sem("pool_seq")
        pcol_ready, sumsq, xn_ready, h_hi, h_lo = (sem(n) for n in (
            "pcol_ready", "sumsq", "xn_ready", "h_hi", "h_lo"))
        sp_in, sp_exp, sp_u, sp_ln, ea_log, adt_ready = (sem(n) for n in (
            "sp_in", "sp_exp", "sp_u", "sp_ln", "ea_log", "adt_ready"))
        dec_ready, hid_ready, kc_ready, gates_ready = (sem(n) for n in (
            "dec_ready", "hid_ready", "kc_ready", "gates_ready"))
        tokn_ready, gcopy_ready = sem("tokn_ready"), sem("gcopy_ready")
        s_fill, s_rel, c_sub, c_exp, pc_ready = (sem(n) for n in (
            "s_fill", "s_rel", "c_sub", "c_exp", "pc_ready"))
        p_exp, p_ready, pv_done = sem("p_exp"), sem("p_ready"), sem("pv_done")
        y_hi, y_lo = sem("y_hi"), sem("y_lo")
        st_done = [sem("st_done0"), sem("st_done1")]
        conv_done, xc_ready = sem("conv_done"), sem("xc_ready")
        am_ready, seg_fill, seg_exp, m_ready, ymm = (sem(n) for n in (
            "am_ready", "seg_fill", "seg_exp", "m_ready", "ymm"))
        xdt_ready, state_ready, yz_ready, ysq_done, yn_rstd, yn_ready = (sem(n) for n in (
            "xdt_ready", "state_ready", "yz_ready", "ysq_done", "yn_rstd", "yn_ready"))
        bar = [sem("phase1_over"), sem("phase2_over"), sem("pre_over")]
        ya_loaded, yb_loaded, xr_loaded = sem("ya_loaded"), sem("yb_loaded"), sem("xr_loaded")
        mrg_ready, m_hi, m_lo = sem("mrg_ready"), sem("m_hi"), sem("m_lo")
        x1_ready, o_ready = sem("x1_ready"), sem("o_ready")
        out_done = [sem("out_done0"), sem("out_done1")]
        silu_u, u_conv, a_ready, a_hi, a_lo = (sem(n) for n in (
            "silu_u", "u_conv", "a_ready", "a_hi", "a_lo"))

        TP, TG = 15, 64
        T_OUT = TP + TG * G
        T_H2 = T_OUT + KD
        T_DN = T_H2 + KD
        K_TOK, K_BACK, K_CMP, K_UNIT, K_XZ, K_BT, K_ST, K_YO, K_Y = 0, 4, 8, 12, 44, 52, 54, 57, 60

        block = ctx.enter_context(nc.Block())

        def w_in_cols(c, n=P):
            return io["w_in"][0, :, c:c + n] if isinstance(c, int) else io["w_in"][0, :, ds(c, n)]

        @block.sync
        def _(sp):
            def load(u, slot, parts):
                if not isinstance(u, int) or u >= 2:
                    if isinstance(u, int):
                        sp.wait_ge(w_lo, u - 1)
                    else:
                        wait_alone(sp, w_lo, u - 1, sp_passed)
                for dst, src in parts:
                    sp.dma_start(dst, src).then_inc(w_loaded[slot], 16)

            def halves(slot, w, kt=8):
                v = w.rearrange("(k p) n -> p k n", p=P)
                h = kt // 2
                return [(wraw[slot][:, 0:h, :], v[:, 0:h, :]), (wraw[slot][:, h:kt, :], v[:, h:kt, :])]

            def sides(slot, w, m, v, n):
                return [(wraw[slot][:, :, 0:m], w.rearrange("(k p) n -> p k n", p=P)),
                        (wraw[slot][:, :, m:m + n], v.rearrange("(k p) n -> p k n", p=P))]

            x_v = io["x"][0].rearrange("(i p) d -> p i d", p=P)
            for i in range(NT):
                sp.dma_start(xt[:, i, :], x_v[:, i, :]).then_inc(x_loaded, 16)
            load(0, 0, sides(0, w_in_cols(C_GATE, 48), 48, w_in_cols(C_DT, 80), 80))
            load(1, 1, halves(1, w_in_cols(C_KC)))
            for q, name in enumerate(("cmp_wk1", "cmp_wv1")):
                sp.dma_start(cw1[q][:, :, :], io[name][0].rearrange("(k p) n -> p k n", p=P)).then_inc(c_loaded, 16)
            for q, name in enumerate(("cmp_wk2", "cmp_wv2")):
                sp.dma_start(cw2[q][:, :, :], io[name][0].rearrange("(k p) n -> p k n", p=P)).then_inc(c_loaded, 16)
            for b in range(2, 5):
                load(b, b % 2, halves(b % 2, w_in_cols(C_KC + P * (b - 1))))
            with sp.Fori(0, G) as g:
                for b in range(GROUP_BLOCKS):
                    u, slot = g * GROUP_BLOCKS + (U_GRP + b), (U_GRP + b) % 2
                    if b < 2:
                        parts = halves(slot, w_in_cols(g * 256 + (C_Q + P * b)))
                    elif b == BKS:
                        parts = sides(slot, w_in_cols(g * DH + C_KS, DH), DH, w_in_cols(g * DH + C_VS, DH), DH)
                    elif b == BKW:
                        parts = sides(slot, w_in_cols(g * DH + C_KW, DH), DH, w_in_cols(g * DH + C_VW, DH), DH)
                    elif b < BB:
                        parts = halves(slot, w_in_cols(g * 512 + (C_X + P * (b - BX))))
                    elif b == BB:
                        parts = halves(slot, w_in_cols(g * P + C_B))
                    elif b == BC:
                        parts = halves(slot, w_in_cols(g * P + C_C))
                    else:
                        parts = halves(slot, w_in_cols(g * 512 + (C_Z + P * (b - BZ))))
                    load(u, slot, parts)

            def merge_units(m, j):
                def cols(w, lo, hi):
                    return w[0, lo:hi, ds(m * P, P)] if not isinstance(m, int) else w[0, lo:hi, m * P:(m + 1) * P]
                srcs = [w_in_cols(m * P + C_GA), cols(io["w_proj_a"], 0, D), w_in_cols(m * P + C_GB),
                        cols(io["w_proj_b"], 0, D), cols(io["w_proj_b"], D, 2 * D)]
                return [(m * 5 + (U_MRG + q), (U_MRG + 5 * j + q) % 2, srcs[q]) for q in range(5)]

            for u, slot, w in merge_units(0, 0)[:2]:
                load(u, slot, halves(slot, w))
            sp.wait_ge(bar[0], 3)
            for i in range(2):
                sp.wait_ge(st_done[i], 32 * (3 * G + 1))
            for q in range(2):
                sp.dma_start(yT[q][:, 0:8, :].bitcast(F32), spill[q, 0:8].rearrange("k p t -> p k t")).then_inc(ya_loaded, 16)
            for q in range(2):
                sp.dma_start(yT[q][:, 8:24, :].bitcast(F32), spill[q, 8:24].rearrange("k p t -> p k t")).then_inc(yb_loaded, 16)
            for u, slot, w in merge_units(0, 0)[2:] + merge_units(1, 1):
                load(u, slot, halves(slot, w))
            with sp.Fori(1, KD // 2) as m2:
                for j in range(2):
                    for u, slot, w in merge_units(m2 * 2 + j, j):
                        load(u, slot, halves(slot, w))

            def out_unit(m, j):
                w = io["w_out"][0, :, ds(m * P, P)] if not isinstance(m, int) else io["w_out"][0, :, m * P:(m + 1) * P]
                load(m + U_OUT, (U_OUT + j) % 2, halves((U_OUT + j) % 2, w))

            out_unit(0, 0)
            out_unit(1, 1)
            sp.wait_ge(bar[1], 3)
            for i in range(NT):
                sp.dma_start(xres[:, i, :], x_v[:, i, :]).then_inc(xr_loaded, 16)
            with sp.Fori(1, KD // 2) as m2:
                out_unit(m2 * 2, 0)
                out_unit(m2 * 2 + 1, 1)
            with sp.Fori(0, FB) as j:
                for q in range(2):
                    slot = (U_UP + q) % 2
                    load(j * 2 + (U_UP + q), slot, halves(slot, io["ffn_w_up"][0, :, ds(j * P + F * q, P)]))
            with sp.Fori(0, KD // 2) as m2:
                for j in range(2):
                    for q in range(3):
                        slot = (U_DN + 3 * j + q) % 2
                        n = 8 if q < 2 else FB - 16
                        load(m2 * 6 + (U_DN + 3 * j + q), slot, halves(
                            slot, io["ffn_w_down"][0, q * D:q * D + n * P, ds((m2 * 2 + j) * P, P)], n))

        @block.gpsimd
        def _(pool):
            seq = Count(pool, pool_seq)
            for tile in (ident[:, :], cmask[:, :], cmask_c[:, :, :]):
                seq.done(nc.gpsimd.memset(tile, 0.0))
            for tile in (tri_le[:, :], gt[:, :], anyvis[:, :]):
                seq.done(nc.gpsimd.memset(tile, 1.0))
            seq.fence()
            nc.gpsimd.affine_select(out=ident[:, :], in_=ident[:, :], compare_op=ALU.not_equal, fill=1.0, base=0,
                                    pattern=[[-1, P]], channel_multiplier=1).then_inc(const_ready, 1)
            nc.gpsimd.affine_select(out=tri_le[:, :], in_=tri_le[:, :], compare_op=ALU.is_ge, fill=0.0, base=0,
                                    pattern=[[1, P]], channel_multiplier=-1).then_inc(const_ready, 1)
            nc.gpsimd.affine_select(out=gt[:, :], in_=gt[:, :], compare_op=ALU.is_gt, fill=0.0, base=0,
                                    pattern=[[-1, P]], channel_multiplier=1).then_inc(const_ready, 1)
            nc.gpsimd.memset(ones[:, :], 1.0).then_inc(const_ready, 1)
            nc.gpsimd.affine_select(out=cmask[:, :], in_=cmask[:, :], compare_op=ALU.is_ge, fill=NEG, base=T - P,
                                    pattern=[[-1, T]], channel_multiplier=1).then_inc(const_ready, 1)
            nc.gpsimd.iota(negdist[:, :], [[1, T]], base=P - T, channel_multiplier=-1,
                           allow_small_or_imprecise_dtypes=True).then_inc(const_ready, 1)
            nc.gpsimd.affine_select(out=cmask_c[:, :, :], in_=cmask_c[:, :, :], compare_op=ALU.is_ge, fill=NEG,
                                    base=-31, pattern=[[P, NT], [-16, NC]], channel_multiplier=1).then_inc(const_ready, 1)
            nc.gpsimd.iota(negdist_c[:, :, :], [[-P, NT], [16, NC]], base=31, channel_multiplier=-1,
                           allow_small_or_imprecise_dtypes=True).then_inc(const_ready, 1)
            nc.gpsimd.affine_select(out=anyvis[:, :], in_=anyvis[:, :], compare_op=ALU.is_ge, fill=0.0,
                                    base=-31, pattern=[[P, NT]], channel_multiplier=1).then_inc(const_ready, 1)

            def lo(u, slot):
                pool.wait_ge(w_hi, u + 1)
                nc.gpsimd.tensor_tensor(wlo[slot][:, :, :], wraw[slot][:, :, :], whi[slot][:, :, :].bitcast(F32),
                                        ALU.subtract).then_inc(w_lo, 1)

            with pool.Fori(0, UNITS // 2) as i:
                lo(i * 2, 0)
                lo(i * 2 + 1, 1)
            lo(UNITS - 1, (UNITS - 1) % 2)

        CONSTS = 9

        @block.tensor
        def _(pe):
            def fill(tau):
                if not isinstance(tau, int) or tau >= 2:
                    pe.wait_ge(t_rel, tau - 1)

            def transposes(tau, par, pieces):
                fill(tau)
                for dst, src in pieces:
                    n = src.shape[0]
                    last = nc.tensor.transpose(dst, src, ident[0:n, 0:n])
                last.then_inc(t_fill, 1)

            def gemm(B, par, units, movs):
                pe.wait_ge(g_rel, B - 1) if (not isinstance(B, int) or B >= 2) else None
                total = sum(n for _, _, n in units)
                k = 0
                for u, slot, n in units:
                    pe.wait_ge(w_lo, u + 1)
                    for kk in range(n):
                        hi, lo = movs[0][:, k, :], movs[1][:, k, :]
                        w, wl = whi[slot][:, kk, :], wlo[slot][:, kk, :]
                        nc.tensor.matmul(gb[par][:, :], w, hi, start=k == 0, stop=False)
                        nc.tensor.matmul(gb[par][:, :], w, lo, start=False, stop=False)
                        ins = nc.tensor.matmul(gb[par][:, :], wl, hi, start=False, stop=k == total - 1)
                        k += 1
                    ins.then_inc(mm_done, 1)

            def pre_gemm(b):
                gemm(b, b % 2, [(b, b % 2, 8)], hT)

            pe.wait_ge(const_ready, CONSTS)
            pe.wait_ge(p_loaded, 16 * 16)
            transposes(0, 0, [(tb[0][:, P * q:P * (q + 1)], prow[:, q, :]) for q in range(3)])
            pe.wait_ge(xn_ready, 1)
            for k in range(KD):
                tau = 1 + k
                transposes(tau, tau % 2, [(tb[tau % 2][:, P * i:P * (i + 1)], xt[:, i, P * k:P * (k + 1)])
                                          for i in range(NT)])
            pe.wait_ge(h_lo, KD)
            for b in range(2):
                pre_gemm(b)
            pe.wait_ge(g_rel, 1)
            transposes(9, 1, [(tb[1][:, P * i:P * (i + 1)], small[:, P * i:P * (i + 1)]) for i in range(NT)])
            pe.wait_ge(c_loaded, 64)
            fill(10)
            for q in range(2):
                for m in range(2):
                    for k in range(16):
                        ins = nc.tensor.matmul(tb[0][:, 2 * q + m:2 * q + m + 1], cw1[q][:, k, P * m:P * (m + 1)],
                                               pcol[:, 1, (PEK, PEV)[q] + k:(PEK, PEV)[q] + k + 1],
                                               start=k == 0, stop=k == 15)
            ins.then_inc(t_fill, 1)
            for b in range(2, 5):
                pre_gemm(b)
            pe.wait_ge(g_rel, 5)
            fill(11)
            for q in range(2):
                for m in range(2):
                    for k in range(16):
                        o = (2 * q + m) * G * NC
                        ins = nc.tensor.matmul(tb[1][:, o:o + G * NC].rearrange("p (g c) -> p g c", g=G),
                                               cw1[q][:, k, P * m:P * (m + 1)],
                                               cst[q][:, :, 2 * k:2 * k + 16 * NC - 15:16], start=k == 0, stop=k == 15)
            ins.then_inc(t_fill, 1)
            pe.wait_ge(hid_ready, 4)
            fill(12)
            for q in range(2):
                for gg in range(G):
                    for m in range(2):
                        o = (q * G + gg) * DH
                        ins = nc.tensor.matmul(tb[0][0:NC, o:o + DH], hid[:, 2 * q + m, NC * gg:NC * (gg + 1)],
                                               cw2[q][:, m, :], start=m == 0, stop=m == 1)
            ins.then_inc(t_fill, 1)
            pe.wait_ge(adt_ready, 1)
            fill(13)
            for q, w in enumerate((tri_le, gt, ones)):
                ins = nc.tensor.matmul(tb[1][:, P * q:P * (q + 1)].rearrange("p (i h) -> p i h", i=NT), w[:, :],
                                       adt[:, :, :], start=True, stop=True)
            ins.then_inc(t_fill, 1)
            pe.wait_ge(kc_ready, 1)
            fill(14)
            for gg in range(G):
                ins = nc.tensor.transpose(tb[0][:, 32 * gg:32 * gg + NC],
                                          kdup[:, gg, :, :].rearrange("p a d -> p (a d)"), ident[0:NC, 0:NC])
            ins.then_inc(t_fill, 1)
            pe.drain().then_inc(bar[2], 1)

            with pe.Fori(0, G) as g:
                def T_(k):
                    return g * TG + (TP + k), (TP + k) % 2

                def grp_gemm(b):
                    i = g * GROUP_BLOCKS + (U_GRP + b)
                    gemm(i, (B_GRP + b) % 2, [(i, (U_GRP + b) % 2, 8)], hT)

                def to_tokens(b):
                    tau, par = T_(K_TOK + b)
                    pe.wait_ge(g_rel, g * GROUP_BLOCKS + (B_GRP + b + 1))
                    transposes(tau, par, [(tb[par][:, P * i:P * (i + 1)], chan[b % 2][:, P * i:P * (i + 1)])
                                          for i in range(NT)])

                for b in (0, 1):
                    grp_gemm(b)
                to_tokens(0)
                grp_gemm(2)
                to_tokens(1)
                grp_gemm(3)
                to_tokens(2)
                to_tokens(3)
                grp_gemm(4)
                grp_gemm(5)
                for b in range(4):
                    tau, par = T_(K_BACK + b)
                    pe.wait_ge(tokn_ready, g * 4 + (b + 1))
                    transposes(tau, par, [(tb[par][:, P * i:P * (i + 1)], tokn[b % 2][:, i, :]) for i in range(NT)])
                pe.wait_ge(t_rel, g * TG + (TP + K_BACK + 4))
                pe.wait_ge(gcopy_ready, g + 1)
                for par, bk in enumerate((s0, s1)):
                    for i in range(NT):
                        for r in (par, par + 2):
                            h = DH * par
                            o = (i * 2 + r // 2) * NC
                            ins = nc.tensor.matmul(bk[:, o:o + NC], qT[r // 2][h:h + DH, P * i:P * (i + 1)],
                                                   kcg[h:h + DH, :], start=True, stop=True)
                    ins.then_inc(s_fill, 1)

                def scores(n):
                    r, br = n // 2, n % 2
                    h = DH * (r % 2)
                    for q, (bk, tiles) in enumerate(((s0, (3,)), (s1, (2,)), (s2, (1, 0)))):
                        if n == 0:
                            pe.wait_ge(s_rel, g * 27 + min(q + 1, 2))
                        else:
                            pe.wait_ge(s_rel, g * 27 + (2 + 3 * (n - 1) + q + 1))
                        for i in tiles:
                            o = 256 if i == 0 else 0
                            ins = nc.tensor.matmul(bk[:, o:o + P * (i + 1)], qT[r // 2][h:h + DH, P * i:P * (i + 1)],
                                                   kT[br][h:h + DH, 0:P * (i + 1)], start=True, stop=True)
                        ins.then_inc(s_fill, 1)

                scores(0)
                for n in range(8):
                    r, br = n // 2, n % 2
                    if n < 7:
                        scores(n + 1)
                    grp_gemm(6 + n)
                    if n == 0:
                        pe.wait_ge(pc_ready, g + 1)
                        for rr in range(R):
                            tau, par = T_(K_CMP + rr)
                            transposes(tau, par, [(tb[par][0:NC, P * i:P * (i + 1)], cs[:, i, rr, :])
                                                  for i in range(NT)])
                    pe.wait_ge(p_ready, g * 8 + (n + 1))
                    for j in range(NT):
                        tau, par = T_(K_UNIT + 4 * n + j)
                        transposes(tau, par, [(tb[par][:, P * (i - j):P * (i - j + 1)],
                                               prob[n % 2][:, off[i] + P * j:off[i] + P * (j + 1)])
                                              for i in range(j, NT)])
                    orow = ob[DH * (r % 2):DH * (r % 2) + DH, :]
                    if br == 0:
                        if n == 0:
                            pe.wait_ge(t_rel, g * TG + (TP + K_CMP + 4))
                        if r == 2:
                            pe.wait_ge(y_hi, g * 6 + 1)
                        nc.tensor.matmul(orow, vcg[:, :], pcT[:, r, :], start=True, stop=False)
                    for j in range(NT):
                        pe.wait_ge(t_rel, g * TG + (TP + K_UNIT + 4 * n + j + 1))
                        w = P * (NT - j)
                        ins = nc.tensor.matmul(orow[:, P * j:T], tok[:, 2 + br, j, DH:P], pT[:, offT[j]:offT[j] + w],
                                               start=False, stop=br == 1 and j == NT - 1)
                    ins.then_inc(pv_done, 1)

                pe.wait_ge(xc_ready, g + 1)
                for c in range(NT):
                    for q, src in enumerate((xc, zchan)):
                        tau, par = T_(K_XZ + 2 * c + q)
                        transposes(tau, par, [(tb[par][:, P * b:P * (b + 1)], src[:, b, P * c:P * (c + 1)])
                                              for b in range(4)])

                def seg(k):
                    pe.wait_ge(am_ready, g * 8 + (k + 1))
                    if k >= 2:
                        pe.wait_ge(seg_exp, g * 8 + (k - 1))
                    for h in range(4):
                        ins = nc.tensor.matmul((s1, s2)[k % 2][:, P * h:P * (h + 1)], amask[k % 2][:, h, :],
                                               tri_le[:, :], start=True, stop=True)
                    ins.then_inc(seg_fill, 1)

                for q in range(2):
                    tau, par = T_(K_BT + q)
                    transposes(tau, par, [(tb[par][:, P * c:P * (c + 1)], xc[:, 4, P * (2 * q + c):P * (2 * q + c + 1)])
                                          for c in range(2)])
                for c in range(NT):
                    ins = nc.tensor.matmul(s0[:, P * c:P * (c + 1)], xc[:, 4, P * c:P * (c + 1)],
                                           xc[:, 5, P * c:P * (c + 1)], start=True, stop=True)
                ins.then_inc(s_fill, 1)
                seg(0)
                seg(1)
                pe.wait_ge(t_rel, g * TG + (TP + K_BT + 2))
                for c in range(3):
                    tau, par = T_(K_ST + c)
                    pe.wait_ge(xdt_ready, g * 4 + (c + 1))
                    fill(tau)
                    nc.tensor.matmul(tb[par][:, :], Bt[:, c, :], xdt2[:, c, :], start=True, stop=True).then_inc(t_fill, 1)
                pe.wait_ge(xdt_ready, g * 4 + 4)
                for k in range(8):
                    c = k // 2
                    yb = (ob, s0)[c % 2]
                    pe.wait_ge(m_ready, g * 8 + (k + 1))
                    if k == 0:
                        pe.wait_ge(y_hi, g * 6 + 2)
                    if k >= 4 and k % 2 == 0:
                        pe.wait_ge(yz_ready, g * 4 + (c - 1))
                    for h in range(4):
                        e = 4 * (k % 2) + h
                        ins = nc.tensor.matmul(yb[:, DH * e:DH * (e + 1)], Ldec[k % 2][:, h, :],
                                               xdt[:, c, DH * e:DH * (e + 1)], start=True, stop=True)
                    ins.then_inc(ymm, 1)
                    if k < 6:
                        seg(k + 2)
                    if k % 2 == 1 and k < 7:
                        cc = c + 1
                        tau, par = T_(K_YO + c)
                        pe.wait_ge(state_ready, g * 3 + cc)
                        fill(tau)
                        nc.tensor.matmul(tb[par][:, :], xc[:, 5, P * cc:P * (cc + 1)], state[:, cc - 1, :],
                                         start=True, stop=True).then_inc(t_fill, 1)
                pe.wait_ge(yn_ready, g * 4 + 4)
                for b in range(4):
                    tau, par = T_(K_Y + b)
                    transposes(tau, par, [(tb[par][:, P * c:P * (c + 1)], zs[:, c, P * b:P * (b + 1)])
                                          for c in range(NT)])
            pe.drain().then_inc(bar[0], 1)

            ya = [y[:, 0:8, :] for y in yT]
            yb_ = [y[:, 8:24, :] for y in yT]

            def merge(m, j):
                def U(q):
                    return (m * 5 + (U_MRG + q), (U_MRG + 5 * j + q) % 2, 8)

                def B(q):
                    return m * 4 + (B_MRG + q), (B_MRG + q) % 2
                gemm(*B(0), [U(0)], hT)
                if isinstance(m, int) and m == 0:
                    pe.wait_ge(ya_loaded, 32)
                gemm(*B(1), [U(1)], ya)
                gemm(*B(2), [U(2)], hT)
                if isinstance(m, int) and m == 0:
                    pe.wait_ge(yb_loaded, 32)
                gemm(*B(3), [U(3), U(4)], yb_)

            merge(0, 0)
            merge(1, 1)
            with pe.Fori(1, KD // 2) as m2:
                merge(m2 * 2, 0)
                merge(m2 * 2 + 1, 1)
            pe.drain().then_inc(bar[1], 1)

            def back(src, tau, par, need):
                pe.wait_ge(g_rel, need)
                transposes(tau, par, [(tb[par][:, P * i:P * (i + 1)], src[:, P * i:P * (i + 1)]) for i in range(NT)])

            pe.wait_ge(m_lo, KD)
            with pe.Fori(0, KD // 2) as m2:
                for j in range(2):
                    gemm(m2 * 2 + (B_OUT + j), (B_OUT + j) % 2, [(m2 * 2 + (U_OUT + j), (U_OUT + j) % 2, 8)], mT)
                for j in range(2):
                    back(ochan[j], m2 * 2 + (T_OUT + j), (T_OUT + j) % 2, m2 * 2 + (B_OUT + j + 1))
            pe.wait_ge(xn_ready, 2)
            for k in range(KD):
                tau = T_H2 + k
                transposes(tau, tau % 2, [(tb[tau % 2][:, P * i:P * (i + 1)], xres[:, i, P * k:P * (k + 1)])
                                          for i in range(NT)])
            pe.wait_ge(h_lo, 2 * KD)
            with pe.Fori(0, FB) as j:
                for q in range(2):
                    gemm(j * 2 + (B_UP + q), (B_UP + q) % 2, [(j * 2 + (U_UP + q), (U_UP + q) % 2, 8)], h2T)
            pe.wait_ge(a_lo, FB)
            with pe.Fori(0, KD // 2) as m2:
                for j in range(2):
                    gemm(m2 * 2 + (B_DN + j), (B_DN + j) % 2,
                         [(m2 * 6 + (U_DN + 3 * j + q), (U_DN + 3 * j + q) % 2, (8, 8, FB - 16)[q]) for q in range(3)], aT)
                    back(ochan[j], m2 * 2 + (T_DN + j), (T_DN + j) % 2, m2 * 2 + (B_DN + j + 1))

        @block.scalar
        def _(act):
            seq = Count(act, act_seq)

            def hi(u, slot):
                if not isinstance(u, int) or u >= 2:
                    act.wait_ge(mm_done, u - 1)
                act.wait_ge(w_loaded[slot], 16 * u + (32 if slot == 0 else 16))
                nc.scalar.activation(whi[slot][:, :, :], wraw[slot][:, :, :], ACT.Copy).then_inc(w_hi, 1)

            def t_wait(tau):
                act.wait_ge(t_fill, tau + 1)

            def split_h(rnd, src_tau, wcol, dst):
                for k in range(KD):
                    tau = src_tau + k
                    t_wait(tau)
                    if k >= 2 or rnd:
                        act.wait_ge(h_lo, rnd * KD + k - 1)
                    nc.scalar.activation(hstage[k % 2][:, :], tb[tau % 2][:, :], ACT.Copy,
                                         scale=pcol[:, 2, wcol + k:wcol + k + 1]).then_inc(t_rel, 1)
                    act.wait_ge(t_rel, tau + 1)
                    nc.scalar.activation(dst[0][:, k, :], hstage[k % 2][:, :], ACT.Copy).then_inc(h_hi, 1)

            act.wait_ge(prow_zero, 1)
            cw, fw = io["ssm_conv_w"][0], io["ffn_conv_w"][0]
            rows = [(0, CW, cw.rearrange("w (b p) -> (w b) p", p=P), 96),
                    (0, CB_, io["ssm_conv_b"].rearrange("l (b p) -> (l b) p", p=P), 24),
                    (1, FW01, fw[0:2].rearrange("w (b p) -> (w b) p", p=P), 88),
                    (1, PEK, io["cmp_pe_k"][0].rearrange("(k a) d -> k (a d)", a=2), 16),
                    (1, PEV, io["cmp_pe_v"][0].rearrange("(k a) d -> k (a d)", a=2), 16),
                    (2, FW2, fw[2:3].rearrange("w (b p) -> (w b) p", p=P), 44),
                    (2, FBI, io["ffn_conv_b"].rearrange("l (b p) -> (l b) p", p=P), 44),
                    (2, N1, io["norm1_w"].rearrange("l (b p) -> (l b) p", p=P), 8),
                    (2, N2, io["norm2_w"].rearrange("l (b p) -> (l b) p", p=P), 8),
                    (2, SN, io["ssm_norm_w"].rearrange("l (b p) -> (l b) p", p=P), 16)]
            for q, r0, src, n in rows:
                act.dma_start(prow[r0:r0 + n, q, :], src).then_inc(p_loaded, 16)
            for half in range(2):
                cols = slice(DH * half, DH * (half + 1))
                act.dma_start(prow[QG:QG + 1, 0, cols], io["nsa_q_gain"]).then_inc(p_loaded, 16)
                act.dma_start(prow[KG:KG + 3, 0, cols], io["nsa_k_gain"][0]).then_inc(p_loaded, 16)
            for q, name in enumerate(("ssm_dt_bias", "ssm_a_log")):
                act.dma_start(drow[:, q, :], io[name].broadcast_to((P, SH))).then_inc(p_loaded, 16)
            act.dma_start(drow[:, 2, :], io["ssm_d"].broadcast_to((P, SH))).then_inc(c_loaded, 16)

            act.wait_ge(x_loaded, 64)
            for i in range(NT):
                ins = nc.scalar.activation(sqj[:, :], xt[:, i, :], ACT.Square, accum_out=stat[:, i:i + 1])
                if i < NT - 1:
                    seq.done(ins)
                    seq.fence()
            ins.then_inc(sumsq, 1)
            t_wait(0)
            nc.scalar.activation(pcol[:, :, :], tb[0][:, 0:384].rearrange("p (q n) -> p q n", q=3), ACT.Copy).then_inc(t_rel, 1)
            act.wait_ge(t_rel, 1)
            hi(0, 0)
            hi(1, 1)
            split_h(0, 1, N1, hT)

            act.wait_ge(p_loaded, 16 * 16)
            nc.scalar.activation(spt[5][:, 0, :], drow[:, 1, :], ACT.Exp).then_inc(ea_log, 1)
            hi(2, 0)
            act.wait_ge(mm_done, 1)
            nc.scalar.activation(small[:, :], gb[0][:, :], ACT.Copy).then_inc(g_rel, 1)

            def stack_tokens(b):
                act.wait_ge(mm_done, b + 1)
                q, blk = (b - 1) // 2, (b - 1) % 2
                src = gb[b % 2]
                for half in range(2):
                    rows_ = src[DH * half:DH * (half + 1), :]
                    gg = 2 * blk + half
                    seq.done(nc.scalar.activation(cst[q][0:DH, gg, :], rows_, ACT.Copy))
                    ins_ = nc.scalar.activation(cst[q][DH:P, gg, 0:T - 1], rows_[:, 1:T], ACT.Copy)
                    if half == 0:
                        seq.done(ins_)
                ins_.then_inc(g_rel, 1)

            hi(3, 1)
            stack_tokens(1)
            t_wait(9)
            seq.done(nc.scalar.activation(gates[:, :, :], tb[1][:, :].rearrange("p (i n) -> p i n", i=NT)[:, :, 0:48],
                                          ACT.Sigmoid))
            nc.scalar.activation(spt[0][:, :, :], tb[1][:, :].rearrange("p (i n) -> p i n", i=NT)[:, :, 48:80],
                                 ACT.Copy).then_inc(t_rel, 1)
            t_wait(10)
            nc.scalar.activation(pebias[:, :], tb[0][:, 0:4], ACT.Copy).then_inc(t_rel, 1)
            for b in range(2, 5):
                hi(b + 2, b % 2)
                stack_tokens(b)
            act.wait_ge(sp_in, 1)
            nc.scalar.activation(spt[1][:, :, :], spt[1][:, :, :], ACT.Exp).then_inc(sp_exp, 1)
            act.wait_ge(sp_u, 1)
            nc.scalar.activation(spt[3][:, :, :], spt[2][:, :, :], ACT.Ln).then_inc(sp_ln, 1)
            t_wait(11)
            act.wait_ge(t_rel, 11)
            for q in range(4):
                ins = nc.scalar.activation(hid[:, q, :], tb[1][:, q * G * NC:(q + 1) * G * NC], ACT.Silu,
                                           bias=pebias[:, q:q + 1])
                ins.then_inc(hid_ready, 1)
            act.wait_ge(hid_ready, 4)
            act.sem_inc(t_rel, 1)
            t_wait(12)
            nc.scalar.activation(kv_c[:, :, :, :].rearrange("p q g d -> p (q g d)"), tb[0][0:NC, :], ACT.Copy).then_inc(t_rel, 1)
            t_wait(13)
            nc.scalar.activation(dec[:, :, :, :].rearrange("p q i h -> p (q i h)"), tb[1][:, 0:384], ACT.Exp).then_inc(t_rel, 1)
            t_wait(14)
            nc.scalar.activation(kcT[:, :, 0:NC], tb[0][:, 0:P].rearrange("p (g c) -> p g c", g=G)[:, :, 0:NC], ACT.Copy,
                                 scale=pcol[:, 0, KG:KG + 1]).then_inc(t_rel, 1)
            act.drain().then_inc(bar[2], 1)
            act.wait_ge(bar[2], 3)
            for i in range(2):
                act.sem_inc(st_done[i], 32)

            with act.Fori(0, G) as g:
                seq.loop(g, ACT_GRP)

                def T_(k):
                    return g * TG + (TP + k), (TP + k) % 2

                def took(b):
                    u = g * GROUP_BLOCKS + (U_GRP + b)
                    hi(u + 2, (U_GRP + b) % 2)
                    return gb[(B_GRP + b) % 2]

                def evac_tok(b):
                    tau, par = T_(K_TOK + b)
                    t_wait(tau)
                    nc.scalar.activation(tok[:, b, :, :].rearrange("p i n -> p (i n)"), tb[par][:, :], ACT.Copy).then_inc(t_rel, 1)

                def evac_chan(b):
                    src = took(b)
                    nc.scalar.activation(chan[b % 2][:, :], src[:, :], ACT.Copy).then_inc(g_rel, 1)

                def evac_x(b):
                    src = took(b)
                    q = b - BX
                    if q >= 2:
                        act.wait_ge(conv_done, g * 6 + (q - 1))
                    nc.scalar.activation(xraw[q % 2][:, :], src[:, :], ACT.Copy).then_inc(g_rel, 1)

                def evac_z(b):
                    src = took(b)
                    nc.scalar.activation(zchan[:, b - BZ, :], src[:, :], ACT.Copy).then_inc(g_rel, 1)

                evac_chan(0)
                evac_chan(1)
                evac_tok(0)
                evac_chan(2)
                evac_tok(1)
                evac_chan(3)
                evac_tok(2)
                evac_tok(3)
                evac_x(4)
                evac_x(5)
                for b, (dst, gain) in enumerate(((qT[0], QG), (qT[1], QG), (kT[0], KG + 1), (kT[1], KG + 2))):
                    tau, par = T_(K_BACK + b)
                    t_wait(tau)
                    nc.scalar.activation(dst[:, :], tb[par][:, :], ACT.Copy, scale=pcol[:, 0, gain:gain + 1]).then_inc(t_rel, 1)
                act.wait_ge(c_sub, g + 1)
                nc.scalar.activation(cs[:, :, :, :], cs[:, :, :, :], ACT.Exp).then_inc(c_exp, 1)

                def o_copy(pair):
                    act.wait_ge(pv_done, g * 8 + (4 * pair + 4))
                    spill_hi(pair, pair, lambda: nc.scalar.activation(ycopy[:, :], ob[:, :], ACT.Copy))

                def spill_hi(e, buf, make):
                    seq.done(make())
                    act.wait_ge(st_done[buf], g * 96 + 32 * (e // 2 + 1))
                    seq.fence()
                    nc.scalar.activation(ysp[buf][0][:, :], ycopy[:, :], ACT.Copy).then_inc(y_hi, 1)

                def spill_out(e, buf, kt):
                    act.wait_ge(y_lo, g * 6 + (e + 1))
                    for q in range(2):
                        act.dma_start(spill[q, ds(kt, 1)].rearrange("a p t -> p (a t)"), ysp[buf][q][:, :].bitcast(F32)).then_inc(st_done[buf], 16)

                for n in range(8):
                    for i in (3, 2, 1, 0):
                        act.wait_ge(s_rel, g * 27 + (2 + 3 * n + {3: 0, 2: 1, 1: 2, 0: 2}[i] + 1))
                        o, w = off[i], P * (i + 1)
                        nc.scalar.activation(prob[n % 2][:, o:o + w], sneg[n % 2][:, o:o + w], ACT.Exp, scale=-1.0,
                                             bias=negmx[n % 2][:, i:i + 1],
                                             accum_out=rsum[n % 2][:, i:i + 1]).then_inc(p_exp, 1)
                    if n == 4:
                        o_copy(0)
                    if n == 5:
                        spill_out(0, 0, g * 2)
                    b = 6 + n
                    (evac_x if b < BZ else evac_z)(b)
                    if n == 0:
                        for r in range(R):
                            tau, par = T_(K_CMP + r)
                            t_wait(tau)
                            nc.scalar.activation(pcT[:, r, :], tb[par][0:NC, :], ACT.Copy).then_inc(t_rel, 1)
                    for j in range(NT):
                        tau, par = T_(K_UNIT + 4 * n + j)
                        w = P * (NT - j)
                        t_wait(tau)
                        if n > 0 and j == 0:
                            act.wait_ge(pv_done, g * 8 + n)
                        nc.scalar.activation(pT[:, offT[j]:offT[j] + w], tb[par][:, 0:w], ACT.Copy).then_inc(t_rel, 1)
                act.wait_ge(conv_done, g * 6 + 6)
                nc.scalar.activation(xc[:, :, :], xc[:, :, :], ACT.Silu).then_inc(xc_ready, 1)
                o_copy(1)
                for c in range(NT):
                    tau, par = T_(K_XZ + 2 * c)
                    t_wait(tau)
                    nc.scalar.activation(Xt[:, c, :], tb[par][:, :], ACT.Copy).then_inc(t_rel, 1)
                    t_wait(tau + 1)
                    nc.scalar.activation(zs[:, c, :], tb[1 - par][:, :], ACT.Silu).then_inc(t_rel, 1)
                spill_out(1, 1, g * 2 + 1)
                for q in range(2):
                    tau, par = T_(K_BT + q)
                    t_wait(tau)
                    nc.scalar.activation(Bt[:, 2 * q:2 * q + 2, :].rearrange("p c n -> p (c n)"), tb[par][:, 0:256],
                                         ACT.Copy).then_inc(t_rel, 1)

                def seg_e(k):
                    act.wait_ge(seg_fill, g * 8 + (k + 1))
                    if k >= 2:
                        act.wait_ge(ymm, g * 8 + (k - 1))
                    nc.scalar.activation(Ldec[k % 2][:, :, :].rearrange("p h n -> p (h n)"), (s1, s2)[k % 2][:, :],
                                         ACT.Exp).then_inc(seg_exp, 1)

                seg_e(0)
                seg_e(1)
                for c in range(3):
                    tau, par = T_(K_ST + c)
                    t_wait(tau)
                    dst = state[:, 0, :] if c == 0 else stc[:, c - 1, :]
                    nc.scalar.activation(dst, tb[par][:, :], ACT.Copy).then_inc(t_rel, 1)
                for k in range(8):
                    if k < 6:
                        seg_e(k + 2)
                    if k % 2 == 1 and k < 7:
                        tau, par = T_(K_YO + k // 2)
                        t_wait(tau)
                        nc.scalar.activation(yoff[:, k // 2, :], tb[par][:, :], ACT.Copy).then_inc(t_rel, 1)
                    if k >= 3 and k % 2 == 1:
                        c = (k - 3) // 2
                        act.wait_ge(yz_ready, g * 4 + (c + 1))
                        nc.scalar.activation(ycopy[:, :], zs[:, c, :], ACT.Square, accum_out=stat[:, c:c + 1]).then_inc(ysq_done, 1)
                        act.wait_ge(ysq_done, g * 4 + (c + 1))
                act.wait_ge(yz_ready, g * 4 + 4)
                nc.scalar.activation(ycopy[:, :], zs[:, 3, :], ACT.Square, accum_out=stat[:, 3:4]).then_inc(ysq_done, 1)
                act.wait_ge(yn_rstd, g + 1)
                for c in range(NT):
                    nc.scalar.activation(zs[:, c, :], zs[:, c, :], ACT.Copy, scale=rstd[:, c:c + 1]).then_inc(yn_ready, 1)
                act.wait_ge(ysq_done, g * 4 + 4)
                for b in range(4):
                    tau, par = T_(K_Y + b)
                    t_wait(tau)
                    nc.scalar.activation(ycopy[:, :], tb[par][:, :], ACT.Copy,
                                         scale=pcol[:, 2, ds(g * 4 + (SN + b), 1)]).then_inc(t_rel, 1)
                    e = 2 + b
                    act.wait_ge(st_done[b % 2], g * 96 + 32 * (e // 2 + 1))
                    act.wait_ge(t_rel, tau + 1)
                    nc.scalar.activation(ysp[b % 2][0][:, :], ycopy[:, :], ACT.Copy).then_inc(y_hi, 1)
                    spill_out(e, b % 2, g * 4 + (8 + b))
            seq.end(G)
            act.drain().then_inc(bar[0], 1)
            act.wait_ge(bar[0], 3)

            def merge(m, j):
                def took(q, B):
                    hi(m * 5 + (U_MRG + q + 2), (U_MRG + 5 * j + q) % 2)
                    return gb[(B_MRG + B) % 2]
                first = isinstance(m, int) and m == 0
                if not first:
                    act.wait_ge(mrg_ready, m * 2)
                src = took(0, 0)
                nc.scalar.activation(sg[:, 0, :], src[:, :], ACT.Sigmoid).then_inc(g_rel, 1)
                src = took(1, 1)
                nc.scalar.activation(pj[:, 0, :], src[:, :], ACT.Copy).then_inc(g_rel, 1)
                src = took(2, 2)
                nc.scalar.activation(sg[:, 1, :], src[:, :], ACT.Sigmoid).then_inc(g_rel, 1)
                took(3, 3)
                src = took(4, 3)
                nc.scalar.activation(pj[:, 1, :], src[:, :], ACT.Copy).then_inc(g_rel, 1)
                act.wait_ge(mrg_ready, m * 2 + 2)
                dst = mT[0][:, m, :] if isinstance(m, int) else mT[0][:, ds(m, 1), :].rearrange("p a t -> p (a t)")
                nc.scalar.activation(dst, hstage[j][:, :], ACT.Copy).then_inc(m_hi, 1)

            merge(0, 0)
            merge(1, 1)
            with act.Fori(1, KD // 2) as m2:
                merge(m2 * 2, 0)
                merge(m2 * 2 + 1, 1)
            act.drain().then_inc(bar[1], 1)
            act.wait_ge(bar[1], 3)

            with act.Fori(0, KD // 2) as m2:
                for j in range(2):
                    hi(m2 * 2 + (U_OUT + j + 2), (U_OUT + j) % 2)
                    nc.scalar.activation(ochan[j][:, :], gb[(B_OUT + j) % 2][:, :], ACT.Copy).then_inc(g_rel, 1)
                for j in range(2):
                    tau, par = m2 * 2 + (T_OUT + j), (T_OUT + j) % 2
                    t_wait(tau)
                    act.wait_ge(x1_ready, m2 * 2 + (j + 1))
                    nc.scalar.activation(otok[j][:, :, :].rearrange("p i n -> p (i n)"), tb[par][:, :], ACT.Copy).then_inc(t_rel, 1)
            act.wait_ge(x1_ready, KD + 2)
            for i in range(NT):
                if i:
                    seq.fence()
                ins = nc.scalar.activation(u_rw[:, :], x1[:, i, :], ACT.Square, accum_out=stat[:, i:i + 1])
                if i < NT - 1:
                    seq.done(ins)
            ins.then_inc(sumsq, 1)
            split_h(1, T_H2, N2, h2T)

            with act.Fori(0, FB) as j:
                for q in range(2):
                    hi(j * 2 + (U_UP + q + 2), (U_UP + q) % 2)
                    act.wait_ge(u_conv, j * 2 + (q + 1))
                    nc.scalar.activation(u_raw[q][:, :], gb[(B_UP + q) % 2][:, :], ACT.Copy).then_inc(g_rel, 1)
                act.wait_ge(u_conv, j * 2 + 4)
                nc.scalar.activation(u_c[0][:, :], u_c[0][:, :], ACT.Silu).then_inc(silu_u, 1)
                act.wait_ge(a_ready, j + 1)
                nc.scalar.activation(aT[0][:, ds(j, 1), :].rearrange("p a t -> p (a t)"), u_a[:, :], ACT.Copy).then_inc(a_hi, 1)

            def down(m2, final):
                for j in range(2):
                    for q in range(3):
                        if not (final and 3 * j + q >= 4):
                            hi(m2 * 6 + (U_DN + 3 * j + q + 2), (U_DN + 3 * j + q) % 2)
                    act.wait_ge(mm_done, m2 * 6 + (U_DN + 3 * j + 3))
                    nc.scalar.activation(ochan[j][:, :], gb[(B_DN + j) % 2][:, :], ACT.Copy).then_inc(g_rel, 1)
                    tau, par = m2 * 2 + (T_DN + j), (T_DN + j) % 2
                    t_wait(tau)
                    act.wait_ge(o_ready, m2 * 2 + (j + 1))
                    nc.scalar.activation(otok[j][:, :, :].rearrange("p i n -> p (i n)"), tb[par][:, :], ACT.Copy).then_inc(t_rel, 1)
                    act.wait_ge(o_ready, m2 * 2 + (j + 3))
                    m = m2 * 2 + j
                    dst = out[0].rearrange("(i p) d -> p i d", p=P)
                    dst = dst[:, :, m * P:(m + 1) * P] if isinstance(m, int) else dst[:, :, ds(m * P, P)]
                    act.dma_start(dst, otile[j][:, :, :]).then_inc(out_done[j], 16)

            with act.Fori(0, KD // 2 - 1) as m2:
                down(m2, False)
            down(KD // 2 - 1, True)
            for j in range(2):
                act.wait_ge(out_done[j], 16 * (KD // 2 + 1))

        @block.vector
        def _(dve):
            seq = Count(dve, dve_seq)
            V = nc.vector

            def rsqrt(dst, src, n, scale, last=None):
                rows_ = src.shape[0]
                v, y, a = (newton[i][0:rows_, 0:n] for i in range(3))
                seq.done(V.tensor_scalar(v, src, scale, EPS, ALU.mult, ALU.add))
                seq.fence()
                seq.done(V.tensor_scalar(a.bitcast(I32), v.bitcast(I32), 1, None, ALU.logical_shift_right))
                seq.fence()
                seq.done(V.tensor_scalar(y.bitcast(I32), a.bitcast(I32), -1, 0x5F3759DF, ALU.mult, ALU.add))
                for it in range(4):
                    seq.fence()
                    seq.done(V.scalar_tensor_tensor(a, y, -0.5, y, ALU.mult, ALU.mult))
                    seq.fence()
                    seq.done(V.tensor_tensor(a, a, v, ALU.mult))
                    seq.fence()
                    out_ = dst if it == 3 else y
                    ins_ = V.scalar_tensor_tensor(out_, a, 1.5, y, ALU.add, ALU.mult)
                    if it == 3 and last is not None:
                        ins_.then_inc(last, 1)
                    else:
                        seq.done(ins_)
                if last is None:
                    seq.fence()

            def lo_h(rnd, dst):
                for k in range(KD):
                    dve.wait_ge(h_hi, rnd * KD + k + 1)
                    V.tensor_tensor(dst[1][:, k, :], hstage[k % 2][:, :], dst[0][:, k, :].bitcast(F32),
                                    ALU.subtract).then_inc(h_lo, 1)

            def normalise(src, dst):
                for i in range(NT):
                    seq.done(V.tensor_scalar(dst[:, i, :], src[:, i, :], rstd[:, i:i + 1], None, ALU.mult))
                seq.fence()

            V.memset(prow[:, :, :], 0.0).then_inc(prow_zero, 1)
            for h in range(NH):
                seq.done(V.memset(slopes[:, h:h + 1], 2.0 ** (-8.0 * (h + 1) / NH)))
            dve.wait_ge(sumsq, 1)
            rsqrt(rstd[:, 0:NT], stat[:, :], NT, 1.0 / D)
            for i in range(NT):
                ins = V.tensor_scalar(xt[:, i, :], xt[:, i, :], rstd[:, i:i + 1], None, ALU.mult)
                if i < NT - 1:
                    seq.done(ins)
            ins.then_inc(xn_ready, 1)
            dve.wait_ge(t_rel, 1)
            seq.done(V.tensor_scalar(pcol[:, 0, QG:QG + 1], pcol[:, 0, QG:QG + 1], DH ** -0.5, None, ALU.mult))
            lo_h(0, hT)
            dve.wait_ge(t_rel, 10)
            dve.wait_ge(ea_log, 1)
            raw, e, u, lnu, w, al = spt
            seq.done(V.tensor_tensor(raw[:, :, :], raw[:, :, :],
                                     drow[:, 0, :].unsqueeze(1).broadcast_to((P, NT, SH)), ALU.add))
            seq.fence()
            V.scalar_tensor_tensor(e[:, :, :], raw[:, :, :], -1.0, raw[:, :, :], ALU.mult, ALU.min).then_inc(sp_in, 1)
            dve.wait_ge(sp_exp, 1)
            V.tensor_scalar(u[:, :, :], e[:, :, :], 1.0, None, ALU.add).then_inc(sp_u, 1)
            dve.wait_ge(sp_u, 1)
            seq.done(V.scalar_tensor_tensor(w[:, :, :], u[:, :, :], -1.0, e[:, :, :], ALU.add, ALU.subtract))
            seq.done(V.reciprocal(dt_all[:, :, :], u[:, :, :]))
            seq.fence()
            seq.done(V.scalar_tensor_tensor(w[:, :, :], w[:, :, :], -1.0, dt_all[:, :, :], ALU.mult, ALU.mult))
            dve.wait_ge(sp_ln, 1)
            seq.fence()
            seq.done(V.tensor_tensor(w[:, :, :], w[:, :, :], lnu[:, :, :], ALU.add))
            seq.fence()
            seq.done(V.scalar_tensor_tensor(dt_all[:, :, :], raw[:, :, :], 0.0, w[:, :, :], ALU.max, ALU.add))
            seq.fence()
            V.scalar_tensor_tensor(adt[:, :, :], dt_all[:, :, :], -1.0,
                                   al[:, 0, :].unsqueeze(1).broadcast_to((P, NT, SH)), ALU.mult, ALU.mult).then_inc(adt_ready, 1)
            dve.wait_ge(t_rel, 13)
            seq.done(V.tensor_tensor(sq_c[:, :, :], kv_c[:, 0, :, :], kv_c[:, 0, :, :], ALU.mult))
            seq.done(V.tensor_copy(vc_all[:, :, :], kv_c[:, 1, :, :]))
            seq.fence()
            seq.done(V.tensor_reduce(stat[0:NC, :], sq_c[:, :, :], AX.X, ALU.add))
            seq.fence()
            rsqrt(rstd[0:NC, 0:G], stat[0:NC, :], G, 1.0 / DH)
            for a in range(2):
                ins = V.tensor_tensor(kdup[:, :, a, :], kv_c[:, 0, :, :],
                                      rstd[0:NC, 0:G].unsqueeze(2).broadcast_to((NC, G, DH)), ALU.mult)
                if a == 0:
                    seq.done(ins)
            ins.then_inc(kc_ready, 1)
            dve.drain().then_inc(bar[2], 1)
            dve.wait_ge(bar[2], 3)
            dve.wait_ge(const_ready, CONSTS)
            dve.wait_ge(c_loaded, 80)

            with dve.Fori(0, G) as g:
                seq.loop(g, DVE_GRP)

                def rel(k):
                    dve.wait_ge(t_rel, g * TG + (TP + k + 1))

                for b in range(4):
                    rel(K_TOK + b)
                    seq.done(V.tensor_tensor(sq[:, :, :], tok[:, b, :, :], tok[:, b, :, :], ALU.mult))
                    seq.fence()
                    seq.done(V.tensor_reduce(ss[:, b, :].rearrange("p (i a) -> p i a", i=NT),
                                             sq[:, :, :].rearrange("p i (a d) -> p i a d", a=2), AX.X, ALU.add))
                    seq.fence()
                rsqrt(rstd[:, :], ss[:, :, :].rearrange("p b n -> p (b n)"), 32, 1.0 / DH)
                for b in range(4):
                    rs = rstd[:, 8 * b:8 * b + 8].rearrange("p (i a) -> p i a", i=NT)
                    src = tok[:, b, :, :].rearrange("p i (a d) -> p i a d", a=2)
                    if b >= 2:
                        rel(K_BACK + b - 2)
                        for a in range(2):
                            ins = V.tensor_tensor(tokn[b % 2][:, :, DH * a:DH * (a + 1)], src[:, :, 0, :],
                                                  rs[:, :, 0:1].broadcast_to((P, NT, DH)), ALU.mult)
                            if a == 0:
                                seq.done(ins)
                    else:
                        for a in range(2):
                            ins = V.tensor_tensor(tokn[b % 2][:, :, DH * a:DH * (a + 1)], src[:, :, a, :],
                                                  rs[:, :, a:a + 1].broadcast_to((P, NT, DH)), ALU.mult)
                            if a == 0:
                                seq.done(ins)
                    ins.then_inc(tokn_ready, 1)
                seq.done(V.tensor_copy(kcg[:, :], kcT[:, ds(g, 1), 0:NC].rearrange("p a c -> p (a c)")))
                V.tensor_copy(vcg[:, :], vc_all[:, ds(g, 1), :].rearrange("p a c -> p (a c)")).then_inc(gcopy_ready, 1)

                def head_bias(r):
                    seq.done(V.scalar_tensor_tensor(hbias[r % 2][:, :], negdist[:, :], slopes[:, ds(g * R + r, 1)],
                                                    cmask[:, :], ALU.mult, ALU.add))

                def conv(q):
                    col = g * 4 + q if q < 4 else g + (16 if q == 4 else 20)
                    w = [pcol[:, 0, ds(col + (24 * s + CW), 1)] for s in range(4)]
                    x_, y_ = xraw[q % 2], xc[:, q, :]
                    dve.wait_ge(g_rel, g * GROUP_BLOCKS + (B_GRP + BX + q + 1))
                    seq.done(V.tensor_scalar(y_, x_[:, :], w[3], pcol[:, 0, ds(col + CB_, 1)], ALU.mult, ALU.add))
                    for s in range(1, 4):
                        seq.fence()
                        ins_ = V.scalar_tensor_tensor(y_[:, s:T], x_[:, 0:T - s], w[3 - s], y_[:, s:T], ALU.mult, ALU.add)
                        if s < 3:
                            seq.done(ins_)
                    ins_.then_inc(conv_done, 1)

                for r in range(R):
                    seq.done(V.scalar_tensor_tensor(cbias[:, :, r, :], negdist_c[:, :, :], slopes[:, ds(g * R + r, 1)],
                                                    cmask_c[:, :, :], ALU.mult, ALU.add))
                head_bias(0)
                conv(0)
                conv(1)
                seq.fence()
                for par, bk in enumerate((s0, s1)):
                    dve.wait_ge(s_fill, g * 27 + (par + 1))
                    for i in range(NT):
                        ins = V.tensor_tensor(cs[:, i, par:R:2, :], bk[:, 2 * NC * i:2 * NC * (i + 1)].rearrange(
                            "p (r c) -> p r c", r=2), cbias[:, i, par:R:2, :], ALU.add)
                        if i < NT - 1:
                            seq.done(ins)
                    ins.then_inc(s_rel, 1)
                seq.fence()
                dve.wait_ge(s_rel, g * 27 + 2)
                cs3 = cs[:, :, :, :].rearrange("p i r c -> p (i r) c")
                seq.done(V.tensor_reduce(cstat[:, 0, :], cs3, AX.X, ALU.max))
                seq.fence()
                V.tensor_tensor(cs3, cs3, cstat[:, 0, :].unsqueeze(2).broadcast_to((P, NT * R, NC)),
                                ALU.subtract).then_inc(c_sub, 1)

                def ttr(n):
                    r = n // 2
                    for q, (bk, tiles) in enumerate(((s0, (3,)), (s1, (2,)), (s2, (1, 0)))):
                        wait_alone(dve, s_fill, g * 27 + (2 + 3 * n + q + 1), dve_passed)
                        for i in tiles:
                            o, w = 256 if i == 0 else 0, P * (i + 1)
                            ins_ = V.tensor_tensor_reduce(sneg[n % 2][:, off[i]:off[i] + w], bk[:, o:o + w],
                                                          hbias[r % 2][:, P * (3 - i):T], -1.0, 3e38, ALU.add, ALU.min,
                                                          negmx[n % 2][:, i:i + 1])
                        ins_.then_inc(s_rel, 1)

                ttr(0)
                dve.wait_ge(c_exp, g + 1)
                seq.done(V.tensor_reduce(cstat[:, 0, :], cs3, AX.X, ALU.add))
                seq.fence()
                seq.done(V.reciprocal(cstat[:, 1, :], cstat[:, 0, :]))
                gcols = gates[:, :, ds(g * 12, 12)].rearrange("p i (r b) -> p i r b", b=3)
                seq.fence()
                seq.done(V.tensor_tensor(cstat[:, 2, :].rearrange("p (i r) -> p i r", i=NT),
                                         cstat[:, 1, :].rearrange("p (i r) -> p i r", i=NT),
                                         anyvis[:, :].unsqueeze(2).broadcast_to((P, NT, R)), ALU.mult))
                seq.fence()
                seq.done(V.tensor_tensor(cstat[:, 0, :].rearrange("p (i r) -> p i r", i=NT),
                                         cstat[:, 2, :].rearrange("p (i r) -> p i r", i=NT), gcols[:, :, :, 0], ALU.mult))
                seq.fence()
                V.tensor_tensor(cs3, cs3, cstat[:, 0, :].unsqueeze(2).broadcast_to((P, NT * R, NC)),
                                ALU.mult).then_inc(pc_ready, 1)

                def scale(n):
                    r, br = n // 2, n % 2
                    dve.wait_ge(p_exp, g * 32 + (4 * n + 4))
                    seq.done(V.reciprocal(pscale[n % 2][:, :], rsum[n % 2][:, :]))
                    seq.fence()
                    seq.done(V.tensor_tensor(pscale[n % 2][:, :], pscale[n % 2][:, :], gcols[:, :, r, 1 + br], ALU.mult))
                    seq.fence()
                    for i in range(NT):
                        pr = prob[n % 2][:, off[i]:off[i] + P * (i + 1)]
                        ins_ = V.tensor_scalar(pr, pr, pscale[n % 2][:, i:i + 1], None, ALU.mult)
                        if i < NT - 1:
                            seq.done(ins_)
                    ins_.then_inc(p_ready, 1)

                def spill_lo(e, buf):
                    dve.wait_ge(y_hi, g * 6 + (e + 1))
                    V.tensor_tensor(ysp[buf][1][:, :], ycopy[:, :], ysp[buf][0][:, :].bitcast(F32),
                                    ALU.subtract).then_inc(y_lo, 1)

                for n in range(8):
                    scale(n)
                    if n % 2 == 1 and n < 7:
                        head_bias(n // 2 + 1)
                        seq.fence()
                    if n < 7:
                        ttr(n + 1)
                    if n == 4:
                        spill_lo(0, 0)
                    if 6 + n < BZ:
                        conv(2 + n)
                def bc(ap, n=SE, w=DH):
                    return ap.unsqueeze(2).broadcast_to((P, n, w))

                def heads(ap):
                    return ap.rearrange("p (e d) -> p e d", e=SE)

                def am(k):
                    c, half = k // 2, k % 2
                    if k >= 2:
                        dve.wait_ge(seg_fill, g * 8 + (k - 1))
                    V.tensor_tensor(amask[k % 2][:, :, :], gt[:, :].unsqueeze(1).broadcast_to((P, 4, P)),
                                    bc(adt[:, c, ds(g * SE + 4 * half, 4)], 4, P), ALU.mult).then_inc(am_ready, 1)

                am(0)
                am(1)
                spill_lo(1, 1)
                for c in range(NT):
                    rel(K_XZ + 2 * c)
                    ins = V.tensor_tensor(heads(xdt[:, c, :]), heads(Xt[:, c, :]), bc(dt_all[:, c, ds(g * SE, SE)]), ALU.mult)
                    if c < 3:
                        seq.done(ins)
                        seq.fence()
                        ins = V.tensor_tensor(heads(xdt2[:, c, :]), heads(xdt[:, c, :]),
                                              bc(dec[:, 1, c, ds(g * SE, SE)]), ALU.mult)
                    ins.then_inc(xdt_ready, 1)
                dve.wait_ge(s_fill, g * 27 + 27)
                V.tensor_tensor(CBm[:, :, :], s0[:, :].rearrange("p (c n) -> p c n", c=NT),
                                tri_le[:, :].unsqueeze(1).broadcast_to((P, NT, P)), ALU.mult).then_inc(s_rel, 1)
                dve.wait_ge(s_rel, g * 27 + 27)

                def combine(c):
                    dve.wait_ge(ymm, g * 8 + (2 * c + 2))
                    yb = (ob, s0)[c % 2]
                    if c:
                        rel(K_YO + c - 1)
                        seq.done(V.tensor_tensor(heads(yoff[:, c - 1, :]), heads(yoff[:, c - 1, :]),
                                                 bc(dec[:, 0, c, ds(g * SE, SE)]), ALU.mult))
                    seq.done(V.tensor_tensor(heads(Xt[:, c, :]), heads(Xt[:, c, :]), bc(drow[:, 2, ds(g * SE, SE)]), ALU.mult))
                    seq.fence()
                    seq.done(V.tensor_tensor(xdt[:, c, :], yb[:, :], Xt[:, c, :], ALU.add))
                    if c:
                        seq.fence()
                        seq.done(V.tensor_tensor(xdt[:, c, :], xdt[:, c, :], yoff[:, c - 1, :], ALU.add))
                    seq.fence()
                    V.tensor_tensor(zs[:, c, :], xdt[:, c, :], zs[:, c, :], ALU.mult).then_inc(yz_ready, 1)

                for k in range(8):
                    c = k // 2
                    dve.wait_ge(seg_exp, g * 8 + (k + 1))
                    V.tensor_tensor(Ldec[k % 2][:, :, :], Ldec[k % 2][:, :, :],
                                    CBm[:, c:c + 1, :].broadcast_to((P, 4, P)), ALU.mult).then_inc(m_ready, 1)
                    if k < 6:
                        am(k + 2)
                    if k < 3:
                        rel(K_ST + k)
                        if k == 0:
                            V.tensor_copy(rstd[:, 0:1], state[:, 0, 0:1]).then_inc(state_ready, 1)
                        else:
                            seq.done(V.tensor_tensor(heads(state[:, k, :]), heads(state[:, k - 1, :]),
                                                     bc(dec[:, 2, k, ds(g * SE, SE)]), ALU.mult))
                            seq.fence()
                            V.tensor_tensor(state[:, k, :], state[:, k, :], stc[:, k - 1, :], ALU.add).then_inc(state_ready, 1)
                            dve.wait_ge(state_ready, g * 3 + (k + 1))
                    if k >= 3 and k % 2 == 1:
                        combine((k - 3) // 2)
                combine(3)
                dve.wait_ge(ysq_done, g * 4 + 4)
                rsqrt(rstd[:, 0:NT], stat[:, :], NT, 1.0 / 512, last=yn_rstd)
                for b in range(4):
                    spill_lo(2 + b, b % 2)
            seq.end(G)
            dve.drain().then_inc(bar[0], 1)
            dve.wait_ge(bar[0], 3)

            def merge(m, j):
                dve.wait_ge(g_rel, m * 4 + (B_MRG + 2))
                V.tensor_tensor(pj[:, 0, :], pj[:, 0, :], sg[:, 0, :], ALU.mult).then_inc(mrg_ready, 1)
                dve.wait_ge(g_rel, m * 4 + (B_MRG + 4))
                seq.done(V.tensor_tensor(pj[:, 1, :], pj[:, 1, :], sg[:, 1, :], ALU.mult))
                seq.fence()
                dve.wait_ge(mrg_ready, m * 2 + 1)
                V.tensor_tensor(hstage[j][:, :], pj[:, 0, :], pj[:, 1, :], ALU.add).then_inc(mrg_ready, 1)
                dve.wait_ge(m_hi, m + 1)
                sl = (lambda t: t[:, m, :]) if isinstance(m, int) else (
                    lambda t: t[:, ds(m, 1), :].rearrange("p a t -> p (a t)"))
                V.tensor_tensor(sl(mT[1]), hstage[j][:, :], sl(mT[0]).bitcast(F32), ALU.subtract).then_inc(m_lo, 1)

            merge(0, 0)
            merge(1, 1)
            with dve.Fori(1, KD // 2) as m2:
                seq.loop(m2 - 1, 2)
                merge(m2 * 2, 0)
                merge(m2 * 2 + 1, 1)
            seq.end(KD // 2 - 1)
            dve.drain().then_inc(bar[1], 1)
            dve.wait_ge(bar[1], 3)
            dve.sem_inc(x1_ready, 2)
            dve.sem_inc(o_ready, 2)
            dve.sem_inc(u_conv, 2)

            dve.wait_ge(xr_loaded, 64)
            with dve.Fori(0, KD // 2) as m2:
                for j in range(2):
                    dve.wait_ge(t_rel, m2 * 2 + (T_OUT + j + 1))
                    cols = ds((m2 * 2 + j) * P, P)
                    V.tensor_tensor(x1[:, :, cols], otok[j][:, :, :], xres[:, :, cols], ALU.add).then_inc(x1_ready, 1)
            dve.wait_ge(sumsq, 2)
            dve.wait_ge(x1_ready, KD + 2)
            rsqrt(rstd[:, 0:NT], stat[:, :], NT, 1.0 / D)
            for i in range(NT):
                ins = V.tensor_scalar(xres[:, i, :], x1[:, i, :], rstd[:, i:i + 1], None, ALU.mult)
                if i < NT - 1:
                    seq.done(ins)
            ins.then_inc(xn_ready, 1)
            lo_h(1, h2T)

            with dve.Fori(0, FB) as j:
                seq.loop(j, 4)
                for q in range(2):
                    w = [pcol[:, 1, ds(j + (FW01 + 44 * s + FB * q), 1)] for s in range(2)]
                    w.append(pcol[:, 2, ds(j + (FW2 + FB * q), 1)])
                    dve.wait_ge(g_rel, j * 2 + (B_UP + q + 1))
                    seq.done(V.tensor_scalar(u_c[q][:, :], u_raw[q][:, :], w[2], pcol[:, 2, ds(j + (FBI + FB * q), 1)],
                                             ALU.mult, ALU.add))
                    seq.fence()
                    seq.done(V.scalar_tensor_tensor(u_c[q][:, 1:T], u_raw[q][:, 0:T - 1], w[1], u_c[q][:, 1:T],
                                                    ALU.mult, ALU.add))
                    seq.fence()
                    V.scalar_tensor_tensor(u_c[q][:, 2:T], u_raw[q][:, 0:T - 2], w[0], u_c[q][:, 2:T],
                                           ALU.mult, ALU.add).then_inc(u_conv, 1)
                dve.wait_ge(u_conv, j * 2 + 4)
                dve.wait_ge(silu_u, j + 1)
                V.tensor_tensor(u_a[:, :], u_c[0][:, :], u_c[1][:, :], ALU.mult).then_inc(a_ready, 1)
                dve.wait_ge(a_hi, j + 1)
                sl = lambda t: t[:, ds(j, 1), :].rearrange("p a t -> p (a t)")
                V.tensor_tensor(sl(aT[1]), u_a[:, :], sl(aT[0]).bitcast(F32), ALU.subtract).then_inc(a_lo, 1)
                dve.wait_ge(a_lo, j + 1)
            seq.end(FB)
            for j in range(2):
                dve.sem_inc(out_done[j], 16)
            with dve.Fori(0, KD // 2) as m2:
                for j in range(2):
                    dve.wait_ge(t_rel, m2 * 2 + (T_DN + j + 1))
                    dve.wait_ge(out_done[j], m2 * 16 + 16)
                    V.tensor_tensor(otile[j][:, :, :], otok[j][:, :, :], x1[:, :, ds((m2 * 2 + j) * P, P)],
                                    ALU.add).then_inc(o_ready, 1)


_INS = ['x', 'norm1_w', 'w_in', 'nsa_q_gain', 'nsa_k_gain', 'cmp_pe_k', 'cmp_pe_v', 'cmp_wk1', 'cmp_wk2', 'cmp_wv1',
        'cmp_wv2', 'ssm_conv_w', 'ssm_conv_b', 'ssm_dt_bias', 'ssm_a_log', 'ssm_d', 'ssm_norm_w', 'w_proj_a',
        'w_proj_b', 'w_out', 'norm2_w', 'ffn_w_up', 'ffn_conv_w', 'ffn_conv_b', 'ffn_w_down']


def kernel(**inputs):
    import numpy as np
    import concourse.bacc as bacc
    from concourse.bass_utils import run_bass_kernel_spmd

    nc = bacc.Bacc("TRN2", target_bir_lowering=False, num_devices=1)
    arrays, io = {}, {}
    for name in _INS:
        a = np.ascontiguousarray(inputs[name])
        arrays[f"in_{name}"] = a
        io[name] = nc.dram_tensor(f"in_{name}", a.shape, mybir.dt.from_np(a.dtype), kind="ExternalInput").ap()
    out = nc.dram_tensor("out", (1, T, D), F32, kind="ExternalOutput").ap()
    spill = nc.dram_tensor("spill", (2, 24, P, T), F32, kind="Internal").ap()
    program(nc, io, out, spill)
    r = run_bass_kernel_spmd(nc, [arrays], core_ids=[0])
    return r.results[0]["out"]
```

```python
from contextlib import ExitStack

import concourse.bass as bass
from concourse import mybir

F32 = mybir.dt.float32
F32R = mybir.dt.float32r
I32 = mybir.dt.int32
ALU = mybir.AluOpType
ACT = mybir.ActivationFunctionType
AX = mybir.AxisListType
ds = bass.ds

P = 128
T = 512
NT = T // P
D = 1024
KD = D // P
G = 4
R = 4
DH = 64
NH = G * R
NC = (T - 32) // 16 + 1
SH = 32
SE = SH // G
SD = 2048
F = 2816
FB = F // P
EPS = 1e-6
NEG = -1e30

C_Q, C_KC, C_VC, C_KS, C_VS, C_KW, C_VW = 0, 1024, 1280, 1536, 1792, 2048, 2304
C_GATE, C_Z, C_X = 2560, 2608, 4656
C_B, C_C = C_X + SD, C_X + SD + 512
C_DT, C_GA, C_GB = 7728, 7760, 8784

CW, CB_, QG, KG = 0, 96, 120, 121
FW01, PEK, PEV = 0, 88, 104
FW2, FBI, N1, N2, SN = 0, 44, 88, 96, 104

PRE_BLOCKS = 9
GROUP_BLOCKS = 14
GATE_BLOCKS = 2 * KD
U_GRP = B_GRP = PRE_BLOCKS
U_GAT = B_GAT = PRE_BLOCKS + G * GROUP_BLOCKS
U_MRG = B_MRG = U_GAT + GATE_BLOCKS - 4
U_OUT, B_OUT = U_MRG + 3 * KD, B_MRG + 2 * KD
U_UP, B_UP = U_OUT + KD, B_OUT + KD
U_DN, B_DN = U_UP + 2 * FB, B_UP + 2 * FB
UNITS = U_DN + 3 * KD
BX, BB, BC, BZ, BF = 0, 4, 5, 6, 10

DVE_GRP = 130


class Count:

    def __init__(self, eng, sem):
        self.eng, self.sem, self.base, self.k, self.i, self.per = eng, sem, 0, 0, None, 0

    def value(self):
        return self.base + self.k if self.i is None else self.i * self.per + (self.base + self.k)

    def done(self, ins):
        ins.then_inc(self.sem, 1)
        self.k += 1

    def fence(self):
        self.eng.wait_ge(self.sem, self.value())

    def loop(self, i, per):
        self.base, self.k, self.i, self.per = self.base + self.k, 0, i, per

    def end(self, trips):
        assert self.k == self.per, (self.k, self.per)
        self.base, self.k, self.i = self.base + trips * self.per, 0, None


def wait_alone(eng, sem, value, passed):
    eng.wait_ge(sem, value)
    eng.sem_inc(passed, 1)


def program(nc, io, out, spill):
    with ExitStack() as ctx:
        def sb(name, shape, dt=F32, c=ctx):
            return c.enter_context(nc.sbuf_tensor(name, shape, dt))

        def bank(name):
            return ctx.enter_context(nc.psum_tensor(name, [P, 512], F32))

        def sem(name):
            return ctx.enter_context(nc.semaphore(name))

        wraw = [sb(f"wraw{s}", [P, 8, P]) for s in range(2)]
        whi = [sb(f"whi{s}", [P, 8, P], F32R) for s in range(2)]
        wlo = [sb(f"wlo{s}", [P, 8, P], F32R) for s in range(2)]
        ident = sb("ident", [P, P])
        pcol = sb("pcol", [P, 3, P])
        stat = sb("stat", [P, NT])
        rstd = sb("rstd", [P, 32])
        newton = [sb(f"newton{i}", [P, 32]) for i in range(4)]
        hstage = [sb(f"hstage{i}", [P, T]) for i in range(2)]

        ph12 = ExitStack()
        hT = [sb("hT_hi", [P, KD, T], F32R, ph12), sb("hT_lo", [P, KD, T], F32R, ph12)]
        chan = sb("chan", [P, 4, T], c=ph12)
        ph1 = ExitStack()
        tri_le = sb("tri_le", [P, P], c=ph1)
        gt = sb("strict_gt", [P, P], c=ph1)
        ones = sb("ones", [P, P], c=ph1)
        negdist = sb("negdist", [P, T], c=ph1)
        cmask = sb("cmask", [P, T], c=ph1)
        negdist_c = sb("negdist_c", [P, NT, NC], c=ph1)
        cmask_c = sb("cmask_c", [P, NT, NC], c=ph1)
        anyvis = sb("anyvis", [P, NT], c=ph1)
        slopes = sb("slopes", [P, NH], c=ph1)
        gates = sb("gates", [P, NT, 48], c=ph1)
        dt_all = sb("dt_all", [P, NT, SH], c=ph1)
        adt = sb("adt", [P, NT, SH], c=ph1)
        dec = sb("dec", [P, 3, NT, SH], c=ph1)
        drow = sb("drow", [P, 3, SH], c=ph1)
        kcT = sb("kcT", [P, G, 32], c=ph1)
        vc_all = sb("vc_all", [NC, G, DH], c=ph1)

        pre = ExitStack()
        xt = sb("xt", [P, NT, D], c=pre)
        prow = sb("prow", [P, 3, P], c=pre)
        small = sb("small", [P, T], c=pre)
        spt = [sb(f"spt{i}", [P, NT, SH], c=pre) for i in range(6)]
        sqj = sb("sqj", [P, D], c=pre)
        cst = [sb(f"cst{i}", [P, G, T], c=pre) for i in range(2)]
        cw1 = [sb(f"cw1_{i}", [P, 16, 256], c=pre) for i in range(2)]
        cw2 = [sb(f"cw2_{i}", [P, 2, DH], c=pre) for i in range(2)]
        pebias = sb("pebias", [P, 4], c=pre)
        hid = sb("hid", [P, 4, G * NC], c=pre)
        kv_c = sb("kv_c", [NC, 2, G, DH], c=pre)
        sq_c = sb("sq_c", [NC, G, DH], c=pre)
        kdup = sb("kdup", [NC, G, 2, DH], c=pre)
        pre.close()

        tok = sb("tok", [P, 4, NT, P], c=ph1)
        sq = sb("sq", [P, NT, P], c=ph1)
        ss = sb("ss", [P, 4, 8], c=ph1)
        tokn = sb("tokn", [P, 4, NT, P], c=ph1)
        qT = [sb(f"qT{i}", [P, T], c=ph1) for i in range(2)]
        kT = [sb(f"kT{i}", [P, T], c=ph1) for i in range(2)]
        kcg = sb("kcg", [P, 2, NC], c=ph1)
        vcg = sb("vcg", [P, R, DH], c=ph1)
        hbias = [sb(f"hbias{i}", [P, T], c=ph1) for i in range(2)]
        cbias = sb("cbias", [P, NT, R, NC], c=ph1)
        cs = sb("cs", [P, NT, R, 32], c=ph1)
        cstat = sb("cstat", [P, 3, NT * R], c=ph1)
        WID = 1280
        off = {3: 0, 2: 512, 1: 896, 0: 1152}
        negmx = [sb(f"negmx{i}", [P, NT], c=ph1) for i in range(2)]
        rsum = [sb(f"rsum{i}", [P, NT], c=ph1) for i in range(2)]
        pscale = [sb(f"pscale{i}", [P, NT], c=ph1) for i in range(2)]
        offT = [0, 512, 896, 1152]
        junk = sb("junk", [P, T], c=ph1)
        obuf = [sb(f"obuf{i}", [P, T], c=ph1) for i in range(2)]
        xraw = [sb(f"xraw{i}", [P, T], c=ph1) for i in range(2)]
        xc = sb("xc", [P, 6, T], c=ph1)
        zchan = sb("zchan", [P, 4, T], c=ph1)
        amask = [sb(f"amask{i}", [P, 4, P], c=ph1) for i in range(2)]
        Ldec = [sb(f"Ldec{i}", [P, 4, P], c=ph1) for i in range(2)]
        state = sb("state", [P, 3, T], c=ph1)
        stc = sb("stc", [P, 2, T], c=ph1)

        piece_a = sb("piece_a", [P, 2 * WID], c=ph1)
        piece_b = sb("piece_b", [P, 2 * WID], c=ph1)
        piece_c = sb("piece_c", [P, R * T], c=ph1)
        piece_d = sb("piece_d", [P, 3 * T], c=ph1)
        pT = piece_d[:, 0:WID]
        yoff = piece_d[:, :].rearrange("p (c t) -> p c t", c=3)
        sneg = [piece_a[:, WID * i:WID * (i + 1)] for i in range(2)]
        prob = [piece_b[:, WID * i:WID * (i + 1)] for i in range(2)]
        pcT = piece_c[:, 0:T]
        xdt = piece_a[:, 0:NT * T].rearrange("p (c t) -> p c t", c=NT)
        xdt2 = piece_b[:, 0:3 * T].rearrange("p (c t) -> p c t", c=3)
        Bt = piece_b[:, 3 * T:4 * T].rearrange("p (c n) -> p c n", c=NT)
        CBm = piece_b[:, 4 * T:5 * T].rearrange("p (c n) -> p c n", c=NT)
        zs = piece_c[:, :].rearrange("p (c t) -> p c t", c=NT)
        Xt = tok[:, :, :, :].rearrange("p c a n -> p c (a n)")
        ph1.close()

        ph2 = ExitStack()
        sg = sb("sg", [P, GATE_BLOCKS, T], c=ph2)
        yT = [sb("yT_hi", [P, 24, T], F32R, ph2), sb("yT_lo", [P, 24, T], F32R, ph2)]
        mT = hT
        pj = sb("pj", [P, 2, T], c=ph2)
        ph2.close()
        ph12.close()

        ph3 = ExitStack()
        h2T = [sb("h2T_hi", [P, KD, T], F32R, ph3), sb("h2T_lo", [P, KD, T], F32R, ph3)]
        x1 = sb("x1", [P, NT, D], c=ph3)
        xres = sb("xres", [P, NT, D], c=ph3)
        ochan = [sb(f"ochan{i}", [P, T], c=ph3) for i in range(2)]
        otok = [sb(f"otok{i}", [P, NT, P], c=ph3) for i in range(2)]
        otile = [sb(f"otile{i}", [P, NT, P], c=ph3) for i in range(2)]
        u_rw = sb("u_raw", [P, 2 * T], c=ph3)
        u_raw = [u_rw[:, T * i:T * (i + 1)] for i in range(2)]
        u_c = [sb(f"u_c{i}", [P, T], c=ph3) for i in range(2)]
        u_a = sb("u_a", [P, T], c=ph3)
        xsq = u_a[:, :].rearrange("p (i n) -> p i n", i=NT)
        xss = sb("xss", [P, KD, NT], c=ph3)
        aT = [sb("aT_hi", [P, FB, T], F32R, ph3), sb("aT_lo", [P, FB, T], F32R, ph3)]
        ph3.close()

        gb = [bank("g0"), bank("g1")]
        tb = [bank("t0"), bank("t1")]
        s0, s1, s2, ob = bank("s0"), bank("s1"), bank("s2"), bank("ob")

        w_loaded = [sem("w_loaded0"), sem("w_loaded1")]
        w_hi, w_lo, mm_done, g_rel = sem("w_hi"), sem("w_lo"), sem("mm_done"), sem("g_rel")
        x_loaded, p_loaded, c_loaded = sem("x_loaded"), sem("p_loaded"), sem("c_loaded")
        sp_passed, dve_passed = sem("sp_passed"), sem("dve_passed")
        const_ready, prow_zero = sem("const_ready"), sem("prow_zero")
        t_fill, t_rel = sem("t_fill"), sem("t_rel")
        act_seq, dve_seq, pool_seq = sem("act_seq"), sem("dve_seq"), sem("pool_seq")
        pcol_ready, sumsq, xn_ready, h_hi, h_lo = (sem(n) for n in (
            "pcol_ready", "sumsq", "xn_ready", "h_hi", "h_lo"))
        sp_in, sp_exp, sp_u, sp_ln, ea_log, adt_ready = (sem(n) for n in (
            "sp_in", "sp_exp", "sp_u", "sp_ln", "ea_log", "adt_ready"))
        dec_ready, hid_ready, kc_ready, gates_ready = (sem(n) for n in (
            "dec_ready", "hid_ready", "kc_ready", "gates_ready"))
        tokn_ready, gcopy_ready = sem("tokn_ready"), sem("gcopy_ready")
        s_fill, s_rel, c_sub, c_exp, pc_ready = (sem(n) for n in (
            "s_fill", "s_rel", "c_sub", "c_exp", "pc_ready"))
        p_exp, p_ready, pv_done = sem("p_exp"), sem("p_ready"), sem("pv_done")
        y_ready = sem("y_ready")
        o_stored, z_stored = [sem("o_stored0"), sem("o_stored1")], sem("z_stored")
        conv_done, xc_ready = sem("conv_done"), sem("xc_ready")
        am_ready, seg_fill, seg_exp, m_ready, ymm = (sem(n) for n in (
            "am_ready", "seg_fill", "seg_exp", "m_ready", "ymm"))
        xdt_ready, state_ready, yz_ready, ysq_done, yn_rstd, yn_ready = (sem(n) for n in (
            "xdt_ready", "state_ready", "yz_ready", "ysq_done", "yn_rstd", "yn_ready"))
        bar = [sem("phase1_over"), sem("phase2_over"), sem("pre_over")]
        y_loaded = [sem(f"y_loaded{i}") for i in range(6)]
        yT_hi, yT_lo, xr_loaded = sem("yT_hi_done"), sem("yT_lo_done"), sem("xr_loaded")
        mrg_ready, m_hi, m_lo = sem("mrg_ready"), sem("m_hi"), sem("m_lo")
        x2n_ready = [sem("x2n_ready0"), sem("x2n_ready1")]
        x1_ready, x1_rstd, o_ready = sem("x1_ready"), sem("x1_rstd"), sem("o_ready")
        out_done = [sem("out_done0"), sem("out_done1")]
        silu_u, u_conv, a_ready, a_hi, a_lo = (sem(n) for n in (
            "silu_u", "u_conv", "a_ready", "a_hi", "a_lo"))

        TP, TG = 15, 62
        SG = 1 + 8 * 3 + 1
        T_OUT = TP + TG * G
        T_H2 = T_OUT + KD
        T_DN = T_H2 + KD
        K_TOK, K_BACK, K_CMP, K_XZ, K_BT, K_ST, K_YO, K_Y = 0, 4, 12, 42, 50, 52, 55, 58
        K_UNIT = [8, 14, 18, 22, 26, 30, 34, 38]

        block = ctx.enter_context(nc.Block())

        def w_in_cols(c, n=P):
            return io["w_in"][0, :, c:c + n] if isinstance(c, int) else io["w_in"][0, :, ds(c, n)]

        @block.sync
        def _(sp):
            def load(u, slot, parts):
                if not isinstance(u, int) or u >= 2:
                    if isinstance(u, int):
                        sp.wait_ge(w_lo, u - 1)
                    else:
                        wait_alone(sp, w_lo, u - 1, sp_passed)
                for dst, src in parts:
                    sp.dma_start(dst, src).then_inc(w_loaded[slot], 16)

            def halves(slot, w, kt=8):
                v = w.rearrange("(k p) n -> p k n", p=P)
                h = kt // 2
                return [(wraw[slot][:, 0:h, :], v[:, 0:h, :]), (wraw[slot][:, h:kt, :], v[:, h:kt, :])]

            def sides(slot, w, m, v, n):
                return [(wraw[slot][:, :, 0:m], w.rearrange("(k p) n -> p k n", p=P)),
                        (wraw[slot][:, :, m:m + n], v.rearrange("(k p) n -> p k n", p=P))]

            x_v = io["x"][0].rearrange("(i p) d -> p i d", p=P)
            for i in range(NT):
                sp.dma_start(xt[:, i, :], x_v[:, i, :]).then_inc(x_loaded, 16)
            load(0, 0, sides(0, w_in_cols(C_GATE, 48), 48, w_in_cols(C_DT, 80), 80))
            load(1, 1, halves(1, w_in_cols(C_KC)))
            for q, name in enumerate(("cmp_wk1", "cmp_wv1")):
                sp.dma_start(cw1[q][:, :, :], io[name][0].rearrange("(k p) n -> p k n", p=P)).then_inc(c_loaded, 16)
            for q, name in enumerate(("cmp_wk2", "cmp_wv2")):
                sp.dma_start(cw2[q][:, :, :], io[name][0].rearrange("(k p) n -> p k n", p=P)).then_inc(c_loaded, 16)
            for b in range(2, 5):
                load(b, b % 2, halves(b % 2, w_in_cols(C_KC + P * (b - 1))))

            def qkv(u, slot, g, b):
                if b < 2:
                    return load(u, slot, halves(slot, w_in_cols(g * 256 + (C_Q + P * b))))
                k, v = ((C_KS, C_VS), (C_KW, C_VW))[b - 2]
                load(u, slot, sides(slot, w_in_cols(g * DH + k, DH), DH, w_in_cols(g * DH + v, DH), DH))

            def group_loads(g):
                for b in range(BF):
                    u, slot = g * GROUP_BLOCKS + (U_GRP + b), (U_GRP + b) % 2
                    if b < BB:
                        col = g * 512 + (C_X + P * (b - BX))
                    elif b < BZ:
                        col = g * P + (C_B if b == BB else C_C)
                    else:
                        col = g * 512 + (C_Z + P * (b - BZ))
                    load(u, slot, halves(slot, w_in_cols(col)))

            for b in range(4):
                qkv(5 + b, (5 + b) % 2, 0, b)
            with sp.Fori(0, G - 1) as g:
                group_loads(g)
                for b in range(4):
                    qkv(g * GROUP_BLOCKS + (U_GRP + BF + b), (U_GRP + BF + b) % 2, g + 1, b)
            group_loads(G - 1)

            def gate_unit(s, par):
                slot = (U_GAT - 4 + par) % 2
                load(s + (U_GAT - 4), slot, halves(slot, w_in_cols(s * P + C_GA)))

            for s in range(6):
                gate_unit(s, s % 2)
            sp.wait_ge(bar[0], 3)
            for i in range(2):
                sp.wait_ge(o_stored[i], 16 * (G + 1))
            sp.wait_ge(z_stored, 64 * (G + 1))

            def y_back(i):
                sp.dma_start(yT[1][:, 4 * i:4 * i + 4, :].bitcast(F32),
                             spill[4 * i:4 * i + 4].rearrange("k p t -> p k t")).then_inc(y_loaded[i], 16)

            y_back(0)
            for s in range(6, GATE_BLOCKS):
                gate_unit(s, s % 2)
                if s < 11:
                    y_back(s - 5)

            def merge_unit(m, j, q):
                w = (io["w_proj_a"], io["w_proj_b"], io["w_proj_b"])[q][0, D * (q // 2):D * (q // 2 + 1), :]
                w = w[:, m * P:(m + 1) * P] if isinstance(m, int) else w[:, ds(m * P, P)]
                slot = (U_MRG + 3 * j + q) % 2
                load(m * 3 + (U_MRG + q), slot, halves(slot, w))

            with sp.Fori(0, KD // 2) as m2:
                for j in range(2):
                    for q in range(3):
                        merge_unit(m2 * 2 + j, j, q)

            def out_unit(m, j):
                w = io["w_out"][0, :, ds(m * P, P)] if not isinstance(m, int) else io["w_out"][0, :, m * P:(m + 1) * P]
                load(m + U_OUT, (U_OUT + j) % 2, halves((U_OUT + j) % 2, w))

            out_unit(0, 0)
            out_unit(1, 1)
            sp.wait_ge(bar[1], 3)
            for i in range(NT):
                sp.dma_start(xres[:, i, :], x_v[:, i, :]).then_inc(xr_loaded, 16)
            with sp.Fori(1, KD // 2) as m2:
                out_unit(m2 * 2, 0)
                out_unit(m2 * 2 + 1, 1)
            with sp.Fori(0, FB) as j:
                for q in range(2):
                    slot = (U_UP + q) % 2
                    load(j * 2 + (U_UP + q), slot, halves(slot, io["ffn_w_up"][0, :, ds(j * P + F * q, P)]))
            with sp.Fori(0, KD // 2) as m2:
                for j in range(2):
                    for q in range(3):
                        slot = (U_DN + 3 * j + q) % 2
                        n = 8 if q < 2 else FB - 16
                        load(m2 * 6 + (U_DN + 3 * j + q), slot, halves(
                            slot, io["ffn_w_down"][0, q * D:q * D + n * P, ds((m2 * 2 + j) * P, P)], n))

        @block.gpsimd
        def _(pool):
            seq = Count(pool, pool_seq)
            for tile in (ident[:, :], cmask[:, :], cmask_c[:, :, :]):
                seq.done(nc.gpsimd.memset(tile, 0.0))
            for tile in (tri_le[:, :], gt[:, :], anyvis[:, :]):
                seq.done(nc.gpsimd.memset(tile, 1.0))
            seq.fence()
            nc.gpsimd.affine_select(out=ident[:, :], in_=ident[:, :], compare_op=ALU.not_equal, fill=1.0, base=0,
                                    pattern=[[-1, P]], channel_multiplier=1).then_inc(const_ready, 1)
            nc.gpsimd.affine_select(out=tri_le[:, :], in_=tri_le[:, :], compare_op=ALU.is_ge, fill=0.0, base=0,
                                    pattern=[[1, P]], channel_multiplier=-1).then_inc(const_ready, 1)
            nc.gpsimd.affine_select(out=gt[:, :], in_=gt[:, :], compare_op=ALU.is_gt, fill=0.0, base=0,
                                    pattern=[[-1, P]], channel_multiplier=1).then_inc(const_ready, 1)
            nc.gpsimd.memset(ones[:, :], 1.0).then_inc(const_ready, 1)
            nc.gpsimd.affine_select(out=cmask[:, :], in_=cmask[:, :], compare_op=ALU.is_ge, fill=NEG, base=T - P,
                                    pattern=[[-1, T]], channel_multiplier=1).then_inc(const_ready, 1)
            nc.gpsimd.iota(negdist[:, :], [[1, T]], base=P - T, channel_multiplier=-1,
                           allow_small_or_imprecise_dtypes=True).then_inc(const_ready, 1)
            nc.gpsimd.affine_select(out=cmask_c[:, :, :], in_=cmask_c[:, :, :], compare_op=ALU.is_ge, fill=NEG,
                                    base=-31, pattern=[[P, NT], [-16, NC]], channel_multiplier=1).then_inc(const_ready, 1)
            nc.gpsimd.iota(negdist_c[:, :, :], [[-P, NT], [16, NC]], base=31, channel_multiplier=-1,
                           allow_small_or_imprecise_dtypes=True).then_inc(const_ready, 1)
            nc.gpsimd.affine_select(out=anyvis[:, :], in_=anyvis[:, :], compare_op=ALU.is_ge, fill=0.0,
                                    base=-31, pattern=[[P, NT]], channel_multiplier=1).then_inc(const_ready, 1)

            def lo(u, slot):
                pool.wait_ge(w_hi, u + 1)
                nc.gpsimd.tensor_tensor(wlo[slot][:, :, :], wraw[slot][:, :, :], whi[slot][:, :, :].bitcast(F32),
                                        ALU.subtract).then_inc(w_lo, 1)

            with pool.Fori(0, UNITS // 2) as i:
                lo(i * 2, 0)
                lo(i * 2 + 1, 1)
            lo(UNITS - 1, (UNITS - 1) % 2)

        CONSTS = 9

        @block.tensor
        def _(pe):
            def fill(tau):
                if not isinstance(tau, int) or tau >= 2:
                    pe.wait_ge(t_rel, tau - 1)

            def transposes(tau, par, pieces):
                fill(tau)
                for dst, src in pieces:
                    n = src.shape[0]
                    last = nc.tensor.transpose(dst, src, ident[0:n, 0:n])
                last.then_inc(t_fill, 1)

            def gemm(B, par, units, movs, between=None):
                pe.wait_ge(g_rel, B - 1) if (not isinstance(B, int) or B >= 2) else None
                total = sum(n for _, _, n in units)
                k = 0
                for u, slot, n in units:
                    pe.wait_ge(w_lo, u + 1)
                    for kk in range(n):
                        if between and k in between:
                            between[k]()
                        hi, lo = movs[0][:, k, :], movs[1][:, k, :]
                        w, wl = whi[slot][:, kk, :], wlo[slot][:, kk, :]
                        nc.tensor.matmul(gb[par][:, :], w, hi, start=k == 0, stop=False)
                        nc.tensor.matmul(gb[par][:, :], w, lo, start=False, stop=False)
                        ins = nc.tensor.matmul(gb[par][:, :], wl, hi, start=False, stop=k == total - 1)
                        k += 1
                    ins.then_inc(mm_done, 1)

            def pre_gemm(b):
                gemm(b, b % 2, [(b, b % 2, 8)], hT)

            pe.wait_ge(const_ready, CONSTS)
            pe.wait_ge(p_loaded, 16 * 16)
            transposes(0, 0, [(tb[0][:, P * q:P * (q + 1)], prow[:, q, :]) for q in range(3)])
            pe.wait_ge(xn_ready, 1)
            for k in range(KD):
                tau = 1 + k
                transposes(tau, tau % 2, [(tb[tau % 2][:, P * i:P * (i + 1)], xt[:, i, P * k:P * (k + 1)])
                                          for i in range(NT)])
            pe.wait_ge(h_lo, KD)
            for b in range(2):
                pre_gemm(b)
            pe.wait_ge(g_rel, 1)
            transposes(9, 1, [(tb[1][:, P * i:P * (i + 1)], small[:, P * i:P * (i + 1)]) for i in range(NT)])
            pe.wait_ge(c_loaded, 64)
            fill(10)
            for q in range(2):
                for m in range(2):
                    for k in range(16):
                        ins = nc.tensor.matmul(tb[0][:, 2 * q + m:2 * q + m + 1], cw1[q][:, k, P * m:P * (m + 1)],
                                               pcol[:, 1, (PEK, PEV)[q] + k:(PEK, PEV)[q] + k + 1],
                                               start=k == 0, stop=k == 15)
            ins.then_inc(t_fill, 1)
            for b in range(2, 6):
                pre_gemm(b)
            pe.wait_ge(g_rel, 5)
            fill(11)
            for q in range(2):
                for m in range(2):
                    for k in range(16):
                        o = (2 * q + m) * G * NC
                        ins = nc.tensor.matmul(tb[1][:, o:o + G * NC].rearrange("p (g c) -> p g c", g=G),
                                               cw1[q][:, k, P * m:P * (m + 1)],
                                               cst[q][:, :, 2 * k:2 * k + 16 * NC - 15:16], start=k == 0, stop=k == 15)
            ins.then_inc(t_fill, 1)
            pre_gemm(6)
            pe.wait_ge(hid_ready, 4)
            fill(12)
            for q in range(2):
                for gg in range(G):
                    for m in range(2):
                        o = (q * G + gg) * DH
                        ins = nc.tensor.matmul(tb[0][0:NC, o:o + DH], hid[:, 2 * q + m, NC * gg:NC * (gg + 1)],
                                               cw2[q][:, m, :], start=m == 0, stop=m == 1)
            ins.then_inc(t_fill, 1)
            pre_gemm(7)
            pe.wait_ge(adt_ready, 1)
            fill(13)
            for q, w in enumerate((tri_le, gt, ones)):
                ins = nc.tensor.matmul(tb[1][:, P * q:P * (q + 1)].rearrange("p (i h) -> p i h", i=NT), w[:, :],
                                       adt[:, :, :], start=True, stop=True)
            ins.then_inc(t_fill, 1)
            pre_gemm(8)
            pe.wait_ge(kc_ready, 1)
            fill(14)
            for gg in range(G):
                ins = nc.tensor.transpose(tb[0][:, 32 * gg:32 * gg + NC],
                                          kdup[:, gg, :, :].rearrange("p a d -> p (a d)"), ident[0:NC, 0:NC])
            ins.then_inc(t_fill, 1)
            pe.drain().then_inc(bar[2], 1)

            with pe.Fori(0, G) as g:
                def T_(k):
                    return g * TG + (TP + k), (TP + k) % 2

                def grp_gemm(b, between=None):
                    i = g * GROUP_BLOCKS + (U_GRP + b)
                    gemm(i, (B_GRP + b) % 2, [(i, (U_GRP + b) % 2, 8)], hT, between)

                for b in range(4):
                    tau, par = T_(K_TOK + b)
                    pe.wait_ge(g_rel, g * GROUP_BLOCKS + (B_GRP - 4 + b + 1))
                    transposes(tau, par, [(tb[par][:, P * i:P * (i + 1)], chan[:, b, P * i:P * (i + 1)])
                                          for i in range(NT)])
                def backs(bs):
                    for b in bs:
                        tau, par = T_(K_BACK + b)
                        pe.wait_ge(tokn_ready, g * 4 + (b + 1))
                        transposes(tau, par, [(tb[par][:, P * i:P * (i + 1)], tokn[:, b, i, :]) for i in range(NT)])

                grp_gemm(BX)
                grp_gemm(BX + 1, {4: lambda: backs((0, 1)), 6: lambda: backs((2, 3))})
                pe.wait_ge(t_rel, g * TG + (TP + K_BACK + 4))
                pe.wait_ge(gcopy_ready, g + 1)
                for i in range(NT):
                    for pair in range(2):
                        o = (i * 2 + pair) * 2 * NC
                        ins = nc.tensor.matmul(s0[:, o:o + 2 * NC], qT[pair][:, P * i:P * (i + 1)],
                                               kcg[:, :, :].rearrange("p a c -> p (a c)"), start=True, stop=True)
                ins.then_inc(s_fill, 1)

                def scores(n):
                    r, br = n // 2, n % 2
                    h = DH * (r % 2)
                    for q, (bk, tiles) in enumerate(((s0, (3,)), (s1, (2,)), (s2, (1, 0)))):
                        if n == 0:
                            pe.wait_ge(s_rel, g * SG + 1)
                        else:
                            pe.wait_ge(s_rel, g * SG + (1 + 3 * (n - 1) + q + 1))
                        for i in tiles:
                            o = 256 if i == 0 else 0
                            ins = nc.tensor.matmul(bk[:, o:o + P * (i + 1)], qT[r // 2][h:h + DH, P * i:P * (i + 1)],
                                                   kT[br][h:h + DH, 0:P * (i + 1)], start=True, stop=True)
                        ins.then_inc(s_fill, 1)

                scores(0)
                for n in range(8):
                    r, br = n // 2, n % 2
                    if n < 7:
                        scores(n + 1)

                    def comp_transposes():
                        pe.wait_ge(pc_ready, g + 1)
                        for q in range(2):
                            tau, par = T_(K_CMP + q)
                            transposes(tau, par, [(tb[par][:, P * i:P * (i + 1)],
                                                   cs[:, 2 * q + i, :, :].rearrange("p r c -> p (r c)"))
                                                  for i in range(2)])

                    def p_transposes(js):
                        pe.wait_ge(p_ready, g * 8 + (n + 1))
                        for j in js:
                            tau, par = T_(K_UNIT[n] + j)
                            transposes(tau, par, [(tb[par][:, P * (i - j):P * (i - j + 1)],
                                                   prob[n % 2][:, off[i] + P * j:off[i] + P * (j + 1)])
                                                  for i in range(j, NT)])

                    between = {3: lambda: p_transposes((0, 1)), 6: lambda: p_transposes((2, 3))}
                    if n == 1:
                        between[1] = comp_transposes
                    grp_gemm(BX + 2 + n, between)
                    orow = ob[DH * (r % 2):DH * (r % 2) + DH, :]
                    if n == 4:
                        pe.wait_ge(y_ready, g * 6 + 1)
                    for j in range(NT):
                        pe.wait_ge(t_rel, g * TG + (TP + K_UNIT[n] + j + 1))
                        w = P * (NT - j)
                        ins = nc.tensor.matmul(orow[:, P * j:T], tok[:, 2 + br, j, DH:P], pT[:, offT[j]:offT[j] + w],
                                               start=br == 0 and j == 0, stop=False)
                    if br == 1:
                        ins = nc.tensor.matmul(orow, vcg[:, r, :], pcT[:, :], start=False, stop=True)
                    ins.then_inc(pv_done, 1)

                def xz_transposes(c):
                    pe.wait_ge(xc_ready, g + 1)
                    pe.wait_ge(g_rel, g * GROUP_BLOCKS + (B_GRP + BZ + 4))
                    for q, src in enumerate((xc, zchan)):
                        tau, par = T_(K_XZ + 2 * c + q)
                        transposes(tau, par, [(tb[par][:, P * b:P * (b + 1)], src[:, b, P * c:P * (c + 1)])
                                              for b in range(4)])

                grp_gemm(BF, {3: lambda: xz_transposes(0), 4: lambda: xz_transposes(1),
                              6: lambda: xz_transposes(2), 7: lambda: xz_transposes(3)})

                def seg(k):
                    pe.wait_ge(am_ready, g * 8 + (k + 1))
                    if k >= 2:
                        pe.wait_ge(seg_exp, g * 8 + (k - 1))
                    for h in range(4):
                        ins = nc.tensor.matmul((s1, s2)[k % 2][:, P * h:P * (h + 1)], amask[k % 2][:, h, :],
                                               tri_le[:, :], start=True, stop=True)
                    ins.then_inc(seg_fill, 1)

                for q in range(2):
                    tau, par = T_(K_BT + q)
                    transposes(tau, par, [(tb[par][:, P * c:P * (c + 1)], xc[:, 4, P * (2 * q + c):P * (2 * q + c + 1)])
                                          for c in range(2)])
                for c in range(NT):
                    ins = nc.tensor.matmul(s0[:, P * c:P * (c + 1)], xc[:, 4, P * c:P * (c + 1)],
                                           xc[:, 5, P * c:P * (c + 1)], start=True, stop=True)
                ins.then_inc(s_fill, 1)
                seg(0)
                seg(1)
                pe.wait_ge(t_rel, g * TG + (TP + K_BT + 2))
                for c in range(3):
                    tau, par = T_(K_ST + c)
                    pe.wait_ge(xdt_ready, g * 4 + (c + 1))
                    fill(tau)
                    nc.tensor.matmul(tb[par][:, :], Bt[:, c, :], xdt2[:, c, :], start=True, stop=True).then_inc(t_fill, 1)
                grp_gemm(BF + 1)
                pe.wait_ge(xdt_ready, g * 4 + 4)
                for k in range(8):
                    c = k // 2
                    yb = (ob, s0)[c % 2]
                    pe.wait_ge(m_ready, g * 8 + (k + 1))
                    if k == 0:
                        pe.wait_ge(y_ready, g * 6 + 2)
                    if k >= 4 and k % 2 == 0:
                        pe.wait_ge(yz_ready, g * 4 + (c - 1))
                    for h in range(4):
                        e = 4 * (k % 2) + h
                        ins = nc.tensor.matmul(yb[:, DH * e:DH * (e + 1)], Ldec[k % 2][:, h, :],
                                               xdt[:, c, DH * e:DH * (e + 1)], start=True, stop=True)
                    ins.then_inc(ymm, 1)
                    if k < 6:
                        seg(k + 2)
                    if k % 2 == 1 and k < 7:
                        cc = c + 1
                        tau, par = T_(K_YO + c)
                        pe.wait_ge(state_ready, g * 3 + cc)
                        fill(tau)
                        nc.tensor.matmul(tb[par][:, :], xc[:, 5, P * cc:P * (cc + 1)], state[:, cc - 1, :],
                                         start=True, stop=True).then_inc(t_fill, 1)
                grp_gemm(BF + 2)
                grp_gemm(BF + 3)
                pe.wait_ge(yn_ready, g * 4 + 4)
                for b in range(4):
                    tau, par = T_(K_Y + b)
                    transposes(tau, par, [(tb[par][:, P * c:P * (c + 1)], zs[:, c, P * b:P * (b + 1)])
                                          for c in range(NT)])
            pe.drain().then_inc(bar[0], 1)

            ya = [y[:, 0:8, :] for y in yT]
            yb_ = [y[:, 8:24, :] for y in yT]

            for b in range(GATE_BLOCKS - 4):
                gemm(B_GAT + b, (B_GAT + b) % 2, [(U_GAT + b, (U_GAT + b) % 2, 8)], hT)
            pe.wait_ge(yT_lo, 6)
            with pe.Fori(0, KD // 2) as m2:
                for j in range(2):
                    def U(q):
                        return m2 * 6 + (U_MRG + 3 * j + q), (U_MRG + 3 * j + q) % 2, 8
                    gemm(m2 * 4 + (B_MRG + 2 * j), B_MRG % 2, [U(0)], ya)
                    gemm(m2 * 4 + (B_MRG + 2 * j + 1), (B_MRG + 1) % 2, [U(1), U(2)], yb_)
            pe.drain().then_inc(bar[1], 1)

            def back(src, tau, par, need):
                pe.wait_ge(g_rel, need)
                transposes(tau, par, [(tb[par][:, P * i:P * (i + 1)], src[:, P * i:P * (i + 1)]) for i in range(NT)])

            def project(m, j, u0, b0, t0, ntiles, mov, between=None):
                n = len(ntiles)
                between = dict(between or {})
                if not isinstance(m, int) or m:
                    between[3] = lambda: back(ochan[1 - j], m + (t0 - 1), (t0 + j - 1) % 2, m + b0)
                gemm(m + b0, (b0 + j) % 2, [(m * n + (u0 + q), (u0 + n * j + q) % 2, ntiles[q]) for q in range(n)],
                     mov, between)

            def projections(u0, b0, t0, ntiles, mov, between):
                project(0, 0, u0, b0, t0, ntiles, mov, between)
                with pe.Fori(0, KD // 2 - 1) as m2:
                    project(m2 * 2 + 1, 1, u0, b0, t0, ntiles, mov)
                    project(m2 * 2 + 2, 0, u0, b0, t0, ntiles, mov)
                project(KD - 1, 1, u0, b0, t0, ntiles, mov)
                back(ochan[1], t0 + KD - 1, (t0 + KD - 1) % 2, b0 + KD)

            pe.wait_ge(m_lo, KD - 2)
            projections(U_OUT, B_OUT, T_OUT, (8,), mT, {6: lambda: pe.wait_ge(m_lo, KD - 1), 7: lambda: pe.wait_ge(m_lo, KD)})
            for k in range(KD):
                tau = T_H2 + k
                if k in (0, KD // 2):
                    pe.wait_ge(x2n_ready[2 * k // KD], NT)
                transposes(tau, tau % 2, [(tb[tau % 2][:, P * i:P * (i + 1)], xres[:, i, P * k:P * (k + 1)])
                                          for i in range(NT)])
            pe.wait_ge(h_lo, 2 * KD)
            with pe.Fori(0, FB) as j:
                for q in range(2):
                    gemm(j * 2 + (B_UP + q), (B_UP + q) % 2, [(j * 2 + (U_UP + q), (U_UP + q) % 2, 8)], h2T)
            pe.wait_ge(a_lo, FB - 2)
            projections(U_DN, B_DN, T_DN, (8, 8, FB - 16), aT, {FB - 2: lambda: pe.wait_ge(a_lo, FB)})

        @block.scalar
        def _(act):
            seq = Count(act, act_seq)

            def hi(u, slot):
                if not isinstance(u, int) or u >= 2:
                    act.wait_ge(mm_done, u - 1)
                act.wait_ge(w_loaded[slot], 16 * u + (32 if slot == 0 else 16))
                nc.scalar.activation(whi[slot][:, :, :], wraw[slot][:, :, :], ACT.Copy).then_inc(w_hi, 1)

            def t_wait(tau):
                act.wait_ge(t_fill, tau + 1)

            def split_h(rnd, src_tau, wcol, dst):
                for k in range(KD):
                    tau = src_tau + k
                    t_wait(tau)
                    if k >= 2 or rnd:
                        act.wait_ge(h_lo, rnd * KD + k - 1)
                    nc.scalar.activation(hstage[k % 2][:, :], tb[tau % 2][:, :], ACT.Copy,
                                         scale=pcol[:, 2, wcol + k:wcol + k + 1]).then_inc(t_rel, 1)
                    act.wait_ge(t_rel, tau + 1)
                    nc.scalar.activation(dst[0][:, k, :], hstage[k % 2][:, :], ACT.Copy).then_inc(h_hi, 1)

            act.wait_ge(prow_zero, 1)
            cw, fw = io["ssm_conv_w"][0], io["ffn_conv_w"][0]
            rows = [(0, CW, cw.rearrange("w (b p) -> (w b) p", p=P), 96),
                    (0, CB_, io["ssm_conv_b"].rearrange("l (b p) -> (l b) p", p=P), 24),
                    (1, FW01, fw[0:2].rearrange("w (b p) -> (w b) p", p=P), 88),
                    (1, PEK, io["cmp_pe_k"][0].rearrange("(k a) d -> k (a d)", a=2), 16),
                    (1, PEV, io["cmp_pe_v"][0].rearrange("(k a) d -> k (a d)", a=2), 16),
                    (2, FW2, fw[2:3].rearrange("w (b p) -> (w b) p", p=P), 44),
                    (2, FBI, io["ffn_conv_b"].rearrange("l (b p) -> (l b) p", p=P), 44),
                    (2, N1, io["norm1_w"].rearrange("l (b p) -> (l b) p", p=P), 8),
                    (2, N2, io["norm2_w"].rearrange("l (b p) -> (l b) p", p=P), 8),
                    (2, SN, io["ssm_norm_w"].rearrange("l (b p) -> (l b) p", p=P), 16)]
            for q, r0, src, n in rows:
                act.dma_start(prow[r0:r0 + n, q, :], src).then_inc(p_loaded, 16)
            for half in range(2):
                cols = slice(DH * half, DH * (half + 1))
                act.dma_start(prow[QG:QG + 1, 0, cols], io["nsa_q_gain"]).then_inc(p_loaded, 16)
                act.dma_start(prow[KG:KG + 3, 0, cols], io["nsa_k_gain"][0]).then_inc(p_loaded, 16)
            for q, name in enumerate(("ssm_dt_bias", "ssm_a_log")):
                act.dma_start(drow[:, q, :], io[name].broadcast_to((P, SH))).then_inc(p_loaded, 16)
            act.dma_start(drow[:, 2, :], io["ssm_d"].broadcast_to((P, SH))).then_inc(c_loaded, 16)

            act.wait_ge(x_loaded, 64)
            for i in range(NT):
                ins = nc.scalar.activation(sqj[:, :], xt[:, i, :], ACT.Square, accum_out=stat[:, i:i + 1])
                if i < NT - 1:
                    seq.done(ins)
                    seq.fence()
            ins.then_inc(sumsq, 1)
            t_wait(0)
            nc.scalar.activation(pcol[:, :, :], tb[0][:, 0:384].rearrange("p (q n) -> p q n", q=3), ACT.Copy).then_inc(t_rel, 1)
            act.wait_ge(t_rel, 1)
            hi(0, 0)
            hi(1, 1)
            split_h(0, 1, N1, hT)

            act.wait_ge(p_loaded, 16 * 16)
            nc.scalar.activation(spt[5][:, 0, :], drow[:, 1, :], ACT.Exp).then_inc(ea_log, 1)
            hi(2, 0)
            act.wait_ge(mm_done, 1)
            nc.scalar.activation(small[:, :], gb[0][:, :], ACT.Copy).then_inc(g_rel, 1)

            def stack_tokens(b):
                act.wait_ge(mm_done, b + 1)
                q, blk = (b - 1) // 2, (b - 1) % 2
                src = gb[b % 2]
                for half in range(2):
                    rows_ = src[DH * half:DH * (half + 1), :]
                    gg = 2 * blk + half
                    seq.done(nc.scalar.activation(cst[q][0:DH, gg, :], rows_, ACT.Copy))
                    ins_ = nc.scalar.activation(cst[q][DH:P, gg, 0:T - 1], rows_[:, 1:T], ACT.Copy)
                    if half == 0:
                        seq.done(ins_)
                ins_.then_inc(g_rel, 1)

            hi(3, 1)
            stack_tokens(1)
            t_wait(9)
            seq.done(nc.scalar.activation(gates[:, :, :], tb[1][:, :].rearrange("p (i n) -> p i n", i=NT)[:, :, 0:48],
                                          ACT.Sigmoid))
            nc.scalar.activation(spt[0][:, :, :], tb[1][:, :].rearrange("p (i n) -> p i n", i=NT)[:, :, 48:80],
                                 ACT.Copy).then_inc(t_rel, 1)
            t_wait(10)
            nc.scalar.activation(pebias[:, :], tb[0][:, 0:4], ACT.Copy).then_inc(t_rel, 1)
            for b in range(2, 5):
                hi(b + 2, b % 2)
                stack_tokens(b)

            def first_chan(b):
                hi(5 + b + 2, (5 + b) % 2)
                nc.scalar.activation(chan[:, b, :], gb[(5 + b) % 2][:, :], ACT.Copy).then_inc(g_rel, 1)

            act.wait_ge(sp_in, 1)
            nc.scalar.activation(spt[1][:, :, :], spt[1][:, :, :], ACT.Exp).then_inc(sp_exp, 1)
            act.wait_ge(sp_u, 1)
            nc.scalar.activation(spt[3][:, :, :], spt[2][:, :, :], ACT.Ln).then_inc(sp_ln, 1)
            first_chan(0)
            t_wait(11)
            act.wait_ge(t_rel, 11)
            for q in range(4):
                ins = nc.scalar.activation(hid[:, q, :], tb[1][:, q * G * NC:(q + 1) * G * NC], ACT.Silu,
                                           bias=pebias[:, q:q + 1])
                ins.then_inc(hid_ready, 1)
            act.wait_ge(hid_ready, 4)
            act.sem_inc(t_rel, 1)
            first_chan(1)
            t_wait(12)
            nc.scalar.activation(kv_c[:, :, :, :].rearrange("p q g d -> p (q g d)"), tb[0][0:NC, :], ACT.Copy).then_inc(t_rel, 1)
            first_chan(2)
            t_wait(13)
            nc.scalar.activation(dec[:, :, :, :].rearrange("p q i h -> p (q i h)"), tb[1][:, 0:384], ACT.Exp).then_inc(t_rel, 1)
            first_chan(3)
            t_wait(14)
            nc.scalar.activation(kcT[:, :, 0:NC], tb[0][:, 0:P].rearrange("p (g c) -> p g c", g=G)[:, :, 0:NC], ACT.Copy,
                                 scale=pcol[:, 0, KG:KG + 1]).then_inc(t_rel, 1)
            act.drain().then_inc(bar[2], 1)
            act.wait_ge(bar[2], 3)
            act.sem_inc(o_stored[0], 16)
            act.sem_inc(o_stored[1], 16)
            act.sem_inc(z_stored, 64)

            with act.Fori(0, G) as g:
                def T_(k):
                    return g * TG + (TP + k), (TP + k) % 2

                def took(b):
                    u = g * GROUP_BLOCKS + (U_GRP + b)
                    hi(u + 2, (U_GRP + b) % 2)
                    return gb[(B_GRP + b) % 2]

                def evac_tok(b):
                    tau, par = T_(K_TOK + b)
                    t_wait(tau)
                    nc.scalar.activation(tok[:, b, :, :].rearrange("p i n -> p (i n)"), tb[par][:, :], ACT.Copy).then_inc(t_rel, 1)

                def evac_chan(b):
                    src = took(BF + b)
                    nc.scalar.activation(chan[:, b, :], src[:, :], ACT.Copy).then_inc(g_rel, 1)

                def evac_x(b):
                    src = took(b)
                    q = b - BX
                    if q >= 2:
                        act.wait_ge(conv_done, g * 6 + (q - 1))
                    nc.scalar.activation(xraw[q % 2][:, :], src[:, :], ACT.Copy).then_inc(g_rel, 1)

                def evac_z(b):
                    src = took(b)
                    if b == BZ:
                        act.wait_ge(z_stored, g * 64 + 64)
                    nc.scalar.activation(zchan[:, b - BZ, :], src[:, :], ACT.Copy).then_inc(g_rel, 1)

                for b in range(4):
                    evac_tok(b)
                evac_x(BX)
                for b, (dst, gain) in enumerate(((qT[0], QG), (qT[1], QG), (kT[0], KG + 1), (kT[1], KG + 2))):
                    tau, par = T_(K_BACK + b)
                    t_wait(tau)
                    nc.scalar.activation(dst[:, :], tb[par][:, :], ACT.Copy, scale=pcol[:, 0, gain:gain + 1]).then_inc(t_rel, 1)
                evac_x(BX + 1)
                act.wait_ge(c_sub, g + 1)
                cs3 = cs[:, :, :, :].rearrange("p i r c -> p (i r) c")[:, :, 0:NC]
                nc.scalar.activation(cs3, cs3, ACT.Exp).then_inc(c_exp, 1)

                def spill_out(e, kt, dst, make, stored):
                    make(dst).then_inc(y_ready, 1)
                    act.wait_ge(y_ready, g * 6 + (e + 1))
                    if e >= 2:
                        act.sem_inc(t_rel, 1)
                    act.dma_start(spill[ds(kt, 1)].rearrange("a p t -> p (a t)"), dst).then_inc(stored, 16)

                def o_out(pair):
                    act.wait_ge(pv_done, g * 8 + (4 * pair + 4))
                    act.wait_ge(o_stored[pair], g * 16 + 16)
                    spill_out(pair, g * 2 + pair, obuf[pair][:, :],
                              lambda dst: nc.scalar.activation(dst, ob[:, :], ACT.Copy), o_stored[pair])

                def exps(n):
                    for i in (3, 2, 1, 0):
                        act.wait_ge(s_rel, g * SG + (1 + 3 * n + {3: 0, 2: 1, 1: 2, 0: 2}[i] + 1))
                        o, w = off[i], P * (i + 1)
                        nc.scalar.activation(prob[n % 2][:, o:o + w], sneg[n % 2][:, o:o + w], ACT.Exp, scale=-1.0,
                                             bias=negmx[n % 2][:, i:i + 1],
                                             accum_out=rsum[n % 2][:, i:i + 1]).then_inc(p_exp, 1)

                exps(0)
                for n in range(8):
                    if n == 4:
                        o_out(0)
                    if n == 1:
                        for q in range(2):
                            tau, par = T_(K_CMP + q)
                            t_wait(tau)
                            nc.scalar.activation(pcT[:, 256 * q:256 * (q + 1)], tb[par][:, 0:256], ACT.Copy).then_inc(t_rel, 1)
                    for j in range(NT):
                        tau, par = T_(K_UNIT[n] + j)
                        w = P * (NT - j)
                        t_wait(tau)
                        if n > 0 and j == 0:
                            act.wait_ge(pv_done, g * 8 + n)
                        nc.scalar.activation(pT[:, offT[j]:offT[j] + w], tb[par][:, 0:w], ACT.Copy).then_inc(t_rel, 1)
                    if n < 7:
                        exps(n + 1)
                    b = BX + 2 + n
                    (evac_x if b < BZ else evac_z)(b)
                    if n == 6:
                        act.wait_ge(conv_done, g * 6 + 6)
                        nc.scalar.activation(xc[:, :, :], xc[:, :, :], ACT.Silu).then_inc(xc_ready, 1)
                o_out(1)
                for c in range(NT):
                    tau, par = T_(K_XZ + 2 * c)
                    t_wait(tau)
                    nc.scalar.activation(Xt[:, c, :], tb[par][:, :], ACT.Copy).then_inc(t_rel, 1)
                    t_wait(tau + 1)
                    nc.scalar.activation(zs[:, c, :], tb[1 - par][:, :], ACT.Silu).then_inc(t_rel, 1)
                evac_chan(0)
                for q in range(2):
                    tau, par = T_(K_BT + q)
                    t_wait(tau)
                    nc.scalar.activation(Bt[:, 2 * q:2 * q + 2, :].rearrange("p c n -> p (c n)"), tb[par][:, 0:256],
                                         ACT.Copy).then_inc(t_rel, 1)

                def seg_e(k):
                    act.wait_ge(seg_fill, g * 8 + (k + 1))
                    if k >= 2:
                        act.wait_ge(ymm, g * 8 + (k - 1))
                    nc.scalar.activation(Ldec[k % 2][:, :, :].rearrange("p h n -> p (h n)"), (s1, s2)[k % 2][:, :],
                                         ACT.Exp).then_inc(seg_exp, 1)

                seg_e(0)
                seg_e(1)
                for c in range(3):
                    tau, par = T_(K_ST + c)
                    t_wait(tau)
                    dst = state[:, 0, :] if c == 0 else stc[:, c - 1, :]
                    nc.scalar.activation(dst, tb[par][:, :], ACT.Copy).then_inc(t_rel, 1)
                evac_chan(1)
                for k in range(8):
                    if k < 6:
                        seg_e(k + 2)
                    if k % 2 == 1 and k < 7:
                        tau, par = T_(K_YO + k // 2)
                        t_wait(tau)
                        nc.scalar.activation(yoff[:, k // 2, :], tb[par][:, :], ACT.Copy).then_inc(t_rel, 1)
                    if k >= 3 and k % 2 == 1:
                        c = (k - 3) // 2
                        act.wait_ge(yz_ready, g * 4 + (c + 1))
                        nc.scalar.activation(junk[:, :], zs[:, c, :], ACT.Square, accum_out=stat[:, c:c + 1]).then_inc(ysq_done, 1)
                        act.wait_ge(ysq_done, g * 4 + (c + 1))
                act.wait_ge(yz_ready, g * 4 + 4)
                nc.scalar.activation(junk[:, :], zs[:, 3, :], ACT.Square, accum_out=stat[:, 3:4]).then_inc(ysq_done, 1)
                evac_chan(2)
                act.wait_ge(yn_rstd, g + 1)
                for c in range(2):
                    nc.scalar.activation(zs[:, c, :], zs[:, c, :], ACT.Copy, scale=rstd[:, c:c + 1]).then_inc(yn_ready, 1)
                evac_chan(3)
                for b in range(4):
                    tau, par = T_(K_Y + b)
                    t_wait(tau)
                    spill_out(2 + b, g * 4 + (8 + b), zchan[:, b, :], lambda dst: nc.scalar.activation(
                        dst, tb[par][:, :], ACT.Copy, scale=pcol[:, 2, ds(g * 4 + (SN + b), 1)]), z_stored)
            act.drain().then_inc(bar[0], 1)
            act.wait_ge(bar[0], 3)

            act.wait_ge(g_rel, B_GAT)
            nc.scalar.activation(sg[:, 0:4, :], chan[:, :, :], ACT.Sigmoid).then_inc(gates_ready, 1)
            for s in range(4, GATE_BLOCKS):
                u = U_GAT - 4 + s
                hi(u + 2, u % 2)
                nc.scalar.activation(sg[:, s, :], gb[u % 2][:, :], ACT.Sigmoid).then_inc(g_rel, 1)
                if 6 <= s < 12:
                    i = s - 6
                    act.wait_ge(y_loaded[i], 16)
                    nc.scalar.activation(yT[0][:, 4 * i:4 * i + 4, :], yT[1][:, 4 * i:4 * i + 4, :].bitcast(F32),
                                         ACT.Copy).then_inc(yT_hi, 1)
            with act.Fori(0, KD // 2) as m2:
                for j in range(2):
                    m = m2 * 2 + j

                    def took(q):
                        hi(m2 * 6 + (U_MRG + 3 * j + q + 2), (U_MRG + 3 * j + q) % 2)
                    took(0)
                    act.wait_ge(mrg_ready, m * 2 + 2)
                    nc.scalar.activation(pj[:, 0, :], gb[B_MRG % 2][:, :], ACT.Copy).then_inc(g_rel, 1)
                    took(1)
                    took(2)
                    nc.scalar.activation(pj[:, 1, :], gb[(B_MRG + 1) % 2][:, :], ACT.Copy).then_inc(g_rel, 1)
                    act.wait_ge(mrg_ready, m * 2 + 4)
                    nc.scalar.activation(mT[0][:, ds(m, 1), :].rearrange("p a t -> p (a t)"), hstage[j][:, :],
                                         ACT.Copy).then_inc(m_hi, 1)
            act.drain().then_inc(bar[1], 1)
            act.wait_ge(bar[1], 3)

            def o_tokens(m, j, t0, freed):
                t_wait(m + t0)
                act.wait_ge(freed, m + 1)
                nc.scalar.activation(otok[j][:, :, :].rearrange("p i n -> p (i n)"), tb[(t0 + j) % 2][:, :],
                                     ACT.Copy).then_inc(t_rel, 1)

            def o_chan(m, j, b0):
                nc.scalar.activation(ochan[j][:, :], gb[(b0 + j) % 2][:, :], ACT.Copy).then_inc(g_rel, 1)

            def out_block(m, j):
                if not isinstance(m, int) or m:
                    o_tokens(m - 1, 1 - j, T_OUT, x1_ready)
                act.wait_ge(mm_done, m + (U_OUT + 1))
                o_chan(m, j, B_OUT)
                hi(m + (U_OUT + 2), (U_OUT + j) % 2)

            out_block(0, 0)
            with act.Fori(0, KD // 2 - 1) as m2:
                out_block(m2 * 2 + 1, 1)
                out_block(m2 * 2 + 2, 0)
            out_block(KD - 1, 1)
            o_tokens(KD - 1, 1, T_OUT, x1_ready)
            act.wait_ge(x1_rstd, 1)
            for h in range(2):
                for i in (2, 3):
                    cols = slice(D // 2 * h, D // 2 * (h + 1))
                    nc.scalar.activation(xres[:, i, cols], x1[:, i, cols], ACT.Copy, scale=rstd[:, i:i + 1]).then_inc(x2n_ready[h], 1)
            split_h(1, T_H2, N2, h2T)

            with act.Fori(0, FB) as j:
                for q in range(2):
                    hi(j * 2 + (U_UP + q + 2), (U_UP + q) % 2)
                    act.wait_ge(u_conv, j * 2 + (q + 1))
                    nc.scalar.activation(u_raw[q][:, :], gb[(B_UP + q) % 2][:, :], ACT.Copy).then_inc(g_rel, 1)
                act.wait_ge(u_conv, j * 2 + 4)
                nc.scalar.activation(u_c[0][:, :], u_c[0][:, :], ACT.Silu).then_inc(silu_u, 1)
                act.wait_ge(a_ready, j + 1)
                nc.scalar.activation(aT[0][:, ds(j, 1), :].rearrange("p a t -> p (a t)"), u_a[:, :], ACT.Copy).then_inc(a_hi, 1)

            def down(m, j, last):
                if not isinstance(m, int) or m:
                    store(m - 1, 1 - j)
                for q in range(3):
                    act.wait_ge(mm_done, m * 3 + (U_DN + q + 1))
                    if q == 2:
                        o_chan(m, j, B_DN)
                    if not last or q == 0:
                        hi(m * 3 + (U_DN + q + 2), (U_DN + 3 * j + q) % 2)

            def store(m, j):
                o_tokens(m, j, T_DN, o_ready)
                act.wait_ge(o_ready, m + 3)
                dst = out[0].rearrange("(i p) d -> p i d", p=P)
                dst = dst[:, :, m * P:(m + 1) * P] if isinstance(m, int) else dst[:, :, ds(m * P, P)]
                act.dma_start(dst, otile[j][:, :, :]).then_inc(out_done[j], 16)

            down(0, 0, False)
            with act.Fori(0, KD // 2 - 1) as m2:
                down(m2 * 2 + 1, 1, False)
                down(m2 * 2 + 2, 0, False)
            down(KD - 1, 1, True)
            store(KD - 1, 1)
            for j in range(2):
                act.wait_ge(out_done[j], 16 * (KD // 2 + 1))

        @block.vector
        def _(dve):
            seq = Count(dve, dve_seq)
            V = nc.vector

            def rsqrt(dst, src, n, scale, last=None):
                rows_ = src.shape[0]
                v, y, a = (newton[i][0:rows_, 0:n] for i in range(3))
                seq.done(V.tensor_scalar(v, src, scale, EPS, ALU.mult, ALU.add))
                seq.fence()
                seq.done(V.tensor_scalar(a.bitcast(I32), v.bitcast(I32), 1, None, ALU.logical_shift_right))
                seq.fence()
                seq.done(V.tensor_scalar(y.bitcast(I32), a.bitcast(I32), -1, 0x5F3759DF, ALU.mult, ALU.add))
                for it in range(3):
                    seq.fence()
                    seq.done(V.scalar_tensor_tensor(a, y, -0.5, y, ALU.mult, ALU.mult))
                    seq.fence()
                    seq.done(V.tensor_tensor(a, a, v, ALU.mult))
                    seq.fence()
                    out_ = dst if it == 2 else y
                    ins_ = V.scalar_tensor_tensor(out_, a, 1.5, y, ALU.add, ALU.mult)
                    if it == 2 and last is not None:
                        ins_.then_inc(last, 1)
                    else:
                        seq.done(ins_)
                if last is None:
                    seq.fence()

            def lo_h(rnd, dst):
                for k in range(KD):
                    dve.wait_ge(h_hi, rnd * KD + k + 1)
                    V.tensor_tensor(dst[1][:, k, :], hstage[k % 2][:, :], dst[0][:, k, :].bitcast(F32),
                                    ALU.subtract).then_inc(h_lo, 1)

            def normalise(src, dst):
                for i in range(NT):
                    seq.done(V.tensor_scalar(dst[:, i, :], src[:, i, :], rstd[:, i:i + 1], None, ALU.mult))
                seq.fence()

            V.memset(prow[:, :, :], 0.0).then_inc(prow_zero, 1)
            for h in range(NH):
                seq.done(V.memset(slopes[:, h:h + 1], 2.0 ** (-8.0 * (h + 1) / NH)))
            dve.wait_ge(sumsq, 1)
            rsqrt(rstd[:, 0:NT], stat[:, :], NT, 1.0 / D)
            for i in range(NT):
                ins = V.tensor_scalar(xt[:, i, :], xt[:, i, :], rstd[:, i:i + 1], None, ALU.mult)
                if i < NT - 1:
                    seq.done(ins)
            ins.then_inc(xn_ready, 1)
            dve.wait_ge(t_rel, 1)
            seq.done(V.tensor_scalar(pcol[:, 0, QG:QG + 1], pcol[:, 0, QG:QG + 1], DH ** -0.5, None, ALU.mult))
            lo_h(0, hT)
            dve.wait_ge(t_rel, 10)
            dve.wait_ge(ea_log, 1)
            raw, e, u, lnu, w, al = spt
            seq.done(V.tensor_tensor(raw[:, :, :], raw[:, :, :],
                                     drow[:, 0, :].unsqueeze(1).broadcast_to((P, NT, SH)), ALU.add))
            seq.fence()
            V.scalar_tensor_tensor(e[:, :, :], raw[:, :, :], -1.0, raw[:, :, :], ALU.mult, ALU.min).then_inc(sp_in, 1)
            dve.wait_ge(sp_exp, 1)
            V.tensor_scalar(u[:, :, :], e[:, :, :], 1.0, None, ALU.add).then_inc(sp_u, 1)
            dve.wait_ge(sp_u, 1)
            seq.done(V.scalar_tensor_tensor(w[:, :, :], u[:, :, :], -1.0, e[:, :, :], ALU.add, ALU.subtract))
            seq.done(V.reciprocal(dt_all[:, :, :], u[:, :, :]))
            seq.fence()
            seq.done(V.scalar_tensor_tensor(w[:, :, :], w[:, :, :], -1.0, dt_all[:, :, :], ALU.mult, ALU.mult))
            dve.wait_ge(sp_ln, 1)
            seq.fence()
            seq.done(V.tensor_tensor(w[:, :, :], w[:, :, :], lnu[:, :, :], ALU.add))
            seq.fence()
            seq.done(V.scalar_tensor_tensor(dt_all[:, :, :], raw[:, :, :], 0.0, w[:, :, :], ALU.max, ALU.add))
            seq.fence()
            V.scalar_tensor_tensor(adt[:, :, :], dt_all[:, :, :], -1.0,
                                   al[:, 0, :].unsqueeze(1).broadcast_to((P, NT, SH)), ALU.mult, ALU.mult).then_inc(adt_ready, 1)
            dve.wait_ge(t_rel, 13)
            seq.done(V.tensor_tensor(sq_c[:, :, :], kv_c[:, 0, :, :], kv_c[:, 0, :, :], ALU.mult))
            seq.done(V.tensor_copy(vc_all[:, :, :], kv_c[:, 1, :, :]))
            seq.fence()
            seq.done(V.tensor_reduce(stat[0:NC, :], sq_c[:, :, :], AX.X, ALU.add))
            seq.fence()
            rsqrt(rstd[0:NC, 0:G], stat[0:NC, :], G, 1.0 / DH)
            for a in range(2):
                ins = V.tensor_tensor(kdup[:, :, a, :], kv_c[:, 0, :, :],
                                      rstd[0:NC, 0:G].unsqueeze(2).broadcast_to((NC, G, DH)), ALU.mult)
                if a == 0:
                    seq.done(ins)
            ins.then_inc(kc_ready, 1)
            dve.drain().then_inc(bar[2], 1)
            dve.wait_ge(bar[2], 3)
            dve.wait_ge(const_ready, CONSTS)
            dve.wait_ge(c_loaded, 80)
            seq.done(V.memset(cs[:, :, :, :], 0.0))
            seq.done(V.memset(vcg[:, :, :], 0.0))
            seq.done(V.memset(kcg[:, :, :], 0.0))
            seq.fence()

            with dve.Fori(0, G) as g:
                seq.loop(g, DVE_GRP)

                def rel(k):
                    dve.wait_ge(t_rel, g * TG + (TP + k + 1))

                def head_bias(r):
                    seq.done(V.scalar_tensor_tensor(hbias[r % 2][:, :], negdist[:, :], slopes[:, ds(g * R + r, 1)],
                                                    cmask[:, :], ALU.mult, ALU.add))

                def conv(q):
                    col = g * 4 + q if q < 4 else g + (16 if q == 4 else 20)
                    w = [pcol[:, 0, ds(col + (24 * s + CW), 1)] for s in range(4)]
                    x_, y_ = xraw[q % 2], xc[:, q, :]
                    dve.wait_ge(g_rel, g * GROUP_BLOCKS + (B_GRP + BX + q + 1))
                    seq.done(V.tensor_scalar(y_, x_[:, :], w[3], pcol[:, 0, ds(col + CB_, 1)], ALU.mult, ALU.add))
                    for s in range(1, 4):
                        seq.fence()
                        ins_ = V.scalar_tensor_tensor(y_[:, s:T], x_[:, 0:T - s], w[3 - s], y_[:, s:T], ALU.mult, ALU.add)
                        if s < 3:
                            seq.done(ins_)
                    ins_.then_inc(conv_done, 1)

                gcols = gates[:, :, ds(g * 12, 12)].rearrange("p i (r b) -> p i r b", b=3)
                cs3 = cs[:, :, :, :].rearrange("p i r c -> p (i r) c")[:, :, 0:NC]
                for a in range(2):
                    half = slice(DH * a, DH * (a + 1))
                    seq.done(V.tensor_copy(kcg[half, a, :], kcT[half, ds(g, 1), 0:NC].rearrange("p a c -> p (a c)")))
                for r in range(R):
                    ins = V.tensor_copy(vcg[32 * r:32 * r + NC, r, :], vc_all[:, ds(g, 1), :].rearrange("p a c -> p (a c)"))
                    if r < R - 1:
                        seq.done(ins)
                ins.then_inc(gcopy_ready, 1)
                for r in range(R):
                    seq.done(V.scalar_tensor_tensor(cbias[:, :, r, :], negdist_c[:, :, :], slopes[:, ds(g * R + r, 1)],
                                                    cmask_c[:, :, :], ALU.mult, ALU.add))
                head_bias(0)
                for b in range(4):
                    rel(K_TOK + b)
                    seq.done(V.tensor_tensor(sq[:, :, :], tok[:, b, :, :], tok[:, b, :, :], ALU.mult))
                    seq.fence()
                    seq.done(V.tensor_reduce(ss[:, b, :].rearrange("p (i a) -> p i a", i=NT),
                                             sq[:, :, :].rearrange("p i (a d) -> p i a d", a=2), AX.X, ALU.add))
                    seq.fence()
                rsqrt(rstd[:, :], ss[:, :, :].rearrange("p b n -> p (b n)"), 32, 1.0 / DH)
                for b in range(4):
                    rs = rstd[:, 8 * b:8 * b + 8].rearrange("p (i a) -> p i a", i=NT)
                    src = tok[:, b, :, :].rearrange("p i (a d) -> p i a d", a=2)
                    for a in range(2):
                        h = a if b < 2 else 0
                        ins = V.tensor_tensor(tokn[:, b, :, DH * a:DH * (a + 1)], src[:, :, h, :],
                                              rs[:, :, h:h + 1].broadcast_to((P, NT, DH)), ALU.mult)
                        if a == 0:
                            seq.done(ins)
                    ins.then_inc(tokn_ready, 1)
                conv(0)
                seq.fence()
                dve.wait_ge(s_fill, g * SG + 1)
                V.tensor_tensor(cs3, s0[:, 0:NT * R * NC].rearrange("p (n c) -> p n c", c=NC),
                                cbias[:, :, :, :].rearrange("p i r c -> p (i r) c"), ALU.add).then_inc(s_rel, 1)
                dve.wait_ge(s_rel, g * SG + 1)
                seq.done(V.tensor_reduce(cstat[:, 0, :], cs3, AX.X, ALU.max))
                seq.fence()
                V.tensor_tensor(cs3, cs3, cstat[:, 0, :].unsqueeze(2).broadcast_to((P, NT * R, NC)),
                                ALU.subtract).then_inc(c_sub, 1)

                def ttr(n):
                    r = n // 2
                    for q, (bk, tiles) in enumerate(((s0, (3,)), (s1, (2,)), (s2, (1, 0)))):
                        wait_alone(dve, s_fill, g * SG + (1 + 3 * n + q + 1), dve_passed)
                        for i in tiles:
                            o, w = 256 if i == 0 else 0, P * (i + 1)
                            ins_ = V.tensor_tensor_reduce(sneg[n % 2][:, off[i]:off[i] + w], bk[:, o:o + w],
                                                          hbias[r % 2][:, P * (3 - i):T], -1.0, 3e38, ALU.add, ALU.min,
                                                          negmx[n % 2][:, i:i + 1])
                        ins_.then_inc(s_rel, 1)

                def comp_probs():
                    dve.wait_ge(c_exp, g + 1)
                    seq.done(V.tensor_reduce(cstat[:, 0, :], cs3, AX.X, ALU.add))
                    seq.fence()
                    seq.done(V.reciprocal(cstat[:, 1, :], cstat[:, 0, :]))
                    seq.fence()
                    seq.done(V.tensor_tensor(cstat[:, 2, :].rearrange("p (i r) -> p i r", i=NT),
                                             cstat[:, 1, :].rearrange("p (i r) -> p i r", i=NT),
                                             anyvis[:, :].unsqueeze(2).broadcast_to((P, NT, R)), ALU.mult))
                    seq.fence()
                    seq.done(V.tensor_tensor(cstat[:, 0, :].rearrange("p (i r) -> p i r", i=NT),
                                             cstat[:, 2, :].rearrange("p (i r) -> p i r", i=NT), gcols[:, :, :, 0], ALU.mult))
                    seq.fence()
                    V.tensor_tensor(cs3, cs3, cstat[:, 0, :].unsqueeze(2).broadcast_to((P, NT * R, NC)),
                                    ALU.mult).then_inc(pc_ready, 1)

                def scale(n):
                    r, br = n // 2, n % 2
                    dve.wait_ge(p_exp, g * 32 + (4 * n + 4))
                    seq.done(V.reciprocal(pscale[n % 2][:, :], rsum[n % 2][:, :]))
                    seq.fence()
                    seq.done(V.tensor_tensor(pscale[n % 2][:, :], pscale[n % 2][:, :], gcols[:, :, r, 1 + br], ALU.mult))
                    seq.fence()
                    for i in range(NT):
                        pr = prob[n % 2][:, off[i]:off[i] + P * (i + 1)]
                        ins_ = V.tensor_scalar(pr, pr, pscale[n % 2][:, i:i + 1], None, ALU.mult)
                        if i < NT - 1:
                            seq.done(ins_)
                    ins_.then_inc(p_ready, 1)

                ttr(0)
                for n in range(8):
                    scale(n)
                    if n % 2 == 1 and n < 7:
                        head_bias(n // 2 + 1)
                        seq.fence()
                    if n < 7:
                        ttr(n + 1)
                    if n == 0:
                        comp_probs()
                    if n < 5:
                        conv(1 + n)
                def bc(ap, n=SE, w=DH):
                    return ap.unsqueeze(2).broadcast_to((P, n, w))

                def heads(ap):
                    return ap.rearrange("p (e d) -> p e d", e=SE)

                def am(k):
                    c, half = k // 2, k % 2
                    if k >= 2:
                        dve.wait_ge(seg_fill, g * 8 + (k - 1))
                    V.tensor_tensor(amask[k % 2][:, :, :], gt[:, :].unsqueeze(1).broadcast_to((P, 4, P)),
                                    bc(adt[:, c, ds(g * SE + 4 * half, 4)], 4, P), ALU.mult).then_inc(am_ready, 1)

                am(0)
                am(1)
                for c in range(NT):
                    rel(K_XZ + 2 * c)
                    ins = V.tensor_tensor(heads(xdt[:, c, :]), heads(Xt[:, c, :]), bc(dt_all[:, c, ds(g * SE, SE)]), ALU.mult)
                    if c < 3:
                        seq.done(ins)
                        seq.fence()
                        ins = V.tensor_tensor(heads(xdt2[:, c, :]), heads(xdt[:, c, :]),
                                              bc(dec[:, 1, c, ds(g * SE, SE)]), ALU.mult)
                    ins.then_inc(xdt_ready, 1)
                dve.wait_ge(s_fill, g * SG + SG)
                V.tensor_tensor(CBm[:, :, :], s0[:, :].rearrange("p (c n) -> p c n", c=NT),
                                tri_le[:, :].unsqueeze(1).broadcast_to((P, NT, P)), ALU.mult).then_inc(s_rel, 1)
                dve.wait_ge(s_rel, g * SG + SG)

                def combine(c):
                    dve.wait_ge(ymm, g * 8 + (2 * c + 2))
                    yb = (ob, s0)[c % 2]
                    if c:
                        rel(K_YO + c - 1)
                        seq.done(V.tensor_tensor(heads(yoff[:, c - 1, :]), heads(yoff[:, c - 1, :]),
                                                 bc(dec[:, 0, c, ds(g * SE, SE)]), ALU.mult))
                    seq.done(V.tensor_tensor(xdt[:, c, :], yb[:, :], Xt[:, c, :], ALU.add))
                    if c:
                        seq.fence()
                        seq.done(V.tensor_tensor(xdt[:, c, :], xdt[:, c, :], yoff[:, c - 1, :], ALU.add))
                    seq.fence()
                    V.tensor_tensor(zs[:, c, :], xdt[:, c, :], zs[:, c, :], ALU.mult).then_inc(yz_ready, 1)

                for k in range(8):
                    c = k // 2
                    dve.wait_ge(seg_exp, g * 8 + (k + 1))
                    V.tensor_tensor(Ldec[k % 2][:, :, :], Ldec[k % 2][:, :, :],
                                    CBm[:, c:c + 1, :].broadcast_to((P, 4, P)), ALU.mult).then_inc(m_ready, 1)
                    if k < 6:
                        am(k + 2)
                    if k < 3:
                        rel(K_ST + k)
                        if k == 0:
                            V.tensor_copy(rstd[:, 0:1], state[:, 0, 0:1]).then_inc(state_ready, 1)
                        else:
                            seq.done(V.tensor_tensor(heads(state[:, k, :]), heads(state[:, k - 1, :]),
                                                     bc(dec[:, 2, k, ds(g * SE, SE)]), ALU.mult))
                            seq.fence()
                            V.tensor_tensor(state[:, k, :], state[:, k, :], stc[:, k - 1, :], ALU.add).then_inc(state_ready, 1)
                            dve.wait_ge(state_ready, g * 3 + (k + 1))
                    if k == 1:
                        for cc in range(NT):
                            seq.done(V.tensor_tensor(heads(Xt[:, cc, :]), heads(Xt[:, cc, :]),
                                                     bc(drow[:, 2, ds(g * SE, SE)]), ALU.mult))
                        seq.fence()
                    if k >= 3 and k % 2 == 1:
                        combine((k - 3) // 2)
                combine(3)
                dve.wait_ge(ysq_done, g * 4 + 4)
                rsqrt(rstd[:, 0:NT], stat[:, :], NT, 1.0 / 512, last=yn_rstd)
                dve.wait_ge(yn_rstd, g + 1)
                for c in (2, 3):
                    V.tensor_scalar(zs[:, c, :], zs[:, c, :], rstd[:, c:c + 1], None, ALU.mult).then_inc(yn_ready, 1)
            seq.end(G)
            dve.drain().then_inc(bar[0], 1)
            dve.wait_ge(bar[0], 3)

            dve.sem_inc(mrg_ready, 2)
            for i in range(6):
                dve.wait_ge(yT_hi, i + 1)
                part = yT[1][:, 4 * i:4 * i + 4, :]
                V.tensor_tensor(part, part.bitcast(F32), yT[0][:, 4 * i:4 * i + 4, :].bitcast(F32),
                                ALU.subtract).then_inc(yT_lo, 1)
            dve.wait_ge(gates_ready, 1)
            with dve.Fori(0, KD // 2) as m2:
                seq.loop(m2, 2)
                for j in range(2):
                    m = m2 * 2 + j

                    def one(t, k):
                        return t[:, ds(k, 1), :].rearrange("p a t -> p (a t)")
                    dve.wait_ge(g_rel, m2 * 4 + (B_MRG + 2 * j + 1))
                    V.tensor_tensor(pj[:, 0, :], pj[:, 0, :], one(sg, m), ALU.mult).then_inc(mrg_ready, 1)
                    dve.wait_ge(g_rel, m2 * 4 + (B_MRG + 2 * j + 2))
                    seq.done(V.tensor_tensor(pj[:, 1, :], pj[:, 1, :], one(sg, m + KD), ALU.mult))
                    seq.fence()
                    dve.wait_ge(mrg_ready, m * 2 + 3)
                    V.tensor_tensor(hstage[j][:, :], pj[:, 0, :], pj[:, 1, :], ALU.add).then_inc(mrg_ready, 1)
                    dve.wait_ge(m_hi, m + 1)
                    V.tensor_tensor(one(mT[1], m), hstage[j][:, :], one(mT[0], m).bitcast(F32), ALU.subtract).then_inc(m_lo, 1)
            seq.end(KD // 2)
            dve.drain().then_inc(bar[1], 1)
            dve.wait_ge(bar[1], 3)
            dve.sem_inc(x1_ready, 2)
            dve.sem_inc(o_ready, 2)
            dve.sem_inc(u_conv, 2)

            dve.wait_ge(xr_loaded, 64)
            with dve.Fori(0, KD // 2) as m2:
                seq.loop(m2, 4)
                for j in range(2):
                    dve.wait_ge(t_rel, m2 * 2 + (T_OUT + j + 1))
                    cols = ds((m2 * 2 + j) * P, P)
                    V.tensor_tensor(x1[:, :, cols], otok[j][:, :, :], xres[:, :, cols], ALU.add).then_inc(x1_ready, 1)
                    dve.wait_ge(x1_ready, m2 * 2 + (j + 3))
                    seq.done(V.tensor_tensor(xsq[:, :, :], x1[:, :, cols], x1[:, :, cols], ALU.mult))
                    seq.fence()
                    seq.done(V.tensor_reduce(xss[:, ds(m2 * 2 + j, 1), :].rearrange("p a i -> p (a i)"), xsq[:, :, :],
                                             AX.X, ALU.add))
                    seq.fence()
            seq.end(KD // 2)
            seq.done(V.tensor_reduce(stat[:, :], xss[:, :, :].rearrange("p m i -> p i m"), AX.X, ALU.add))
            seq.fence()
            rsqrt(rstd[:, 0:NT], stat[:, :], NT, 1.0 / D, last=x1_rstd)
            dve.wait_ge(x1_rstd, 1)
            for h in range(2):
                for i in (0, 1):
                    cols = slice(D // 2 * h, D // 2 * (h + 1))
                    V.tensor_scalar(xres[:, i, cols], x1[:, i, cols], rstd[:, i:i + 1], None, ALU.mult).then_inc(x2n_ready[h], 1)
            lo_h(1, h2T)

            with dve.Fori(0, FB) as j:
                seq.loop(j, 4)
                for q in range(2):
                    w = [pcol[:, 1, ds(j + (FW01 + 44 * s + FB * q), 1)] for s in range(2)]
                    w.append(pcol[:, 2, ds(j + (FW2 + FB * q), 1)])
                    dve.wait_ge(g_rel, j * 2 + (B_UP + q + 1))
                    seq.done(V.tensor_scalar(u_c[q][:, :], u_raw[q][:, :], w[2], pcol[:, 2, ds(j + (FBI + FB * q), 1)],
                                             ALU.mult, ALU.add))
                    seq.fence()
                    seq.done(V.scalar_tensor_tensor(u_c[q][:, 1:T], u_raw[q][:, 0:T - 1], w[1], u_c[q][:, 1:T],
                                                    ALU.mult, ALU.add))
                    seq.fence()
                    V.scalar_tensor_tensor(u_c[q][:, 2:T], u_raw[q][:, 0:T - 2], w[0], u_c[q][:, 2:T],
                                           ALU.mult, ALU.add).then_inc(u_conv, 1)
                dve.wait_ge(u_conv, j * 2 + 4)
                dve.wait_ge(silu_u, j + 1)
                V.tensor_tensor(u_a[:, :], u_c[0][:, :], u_c[1][:, :], ALU.mult).then_inc(a_ready, 1)
                dve.wait_ge(a_hi, j + 1)
                sl = lambda t: t[:, ds(j, 1), :].rearrange("p a t -> p (a t)")
                V.tensor_tensor(sl(aT[1]), u_a[:, :], sl(aT[0]).bitcast(F32), ALU.subtract).then_inc(a_lo, 1)
                dve.wait_ge(a_lo, j + 1)
            seq.end(FB)
            for j in range(2):
                dve.sem_inc(out_done[j], 16)
            with dve.Fori(0, KD // 2) as m2:
                for j in range(2):
                    dve.wait_ge(t_rel, m2 * 2 + (T_DN + j + 1))
                    dve.wait_ge(out_done[j], m2 * 16 + 16)
                    V.tensor_tensor(otile[j][:, :, :], otok[j][:, :, :], x1[:, :, ds((m2 * 2 + j) * P, P)],
                                    ALU.add).then_inc(o_ready, 1)


_INS = ['x', 'norm1_w', 'w_in', 'nsa_q_gain', 'nsa_k_gain', 'cmp_pe_k', 'cmp_pe_v', 'cmp_wk1', 'cmp_wk2', 'cmp_wv1',
        'cmp_wv2', 'ssm_conv_w', 'ssm_conv_b', 'ssm_dt_bias', 'ssm_a_log', 'ssm_d', 'ssm_norm_w', 'w_proj_a',
        'w_proj_b', 'w_out', 'norm2_w', 'ffn_w_up', 'ffn_conv_w', 'ffn_conv_b', 'ffn_w_down']


def kernel(**inputs):
    import numpy as np
    import concourse.bacc as bacc
    from concourse.bass_utils import run_bass_kernel_spmd

    nc = bacc.Bacc("TRN2", target_bir_lowering=False, num_devices=1)
    arrays, io = {}, {}
    for name in _INS:
        a = np.ascontiguousarray(inputs[name])
        arrays[f"in_{name}"] = a
        io[name] = nc.dram_tensor(f"in_{name}", a.shape, mybir.dt.from_np(a.dtype), kind="ExternalInput").ap()
    out = nc.dram_tensor("out", (1, T, D), F32, kind="ExternalOutput").ap()
    spill = nc.dram_tensor("spill", (24, P, T), F32, kind="Internal").ap()
    program(nc, io, out, spill)
    r = run_bass_kernel_spmd(nc, [arrays], core_ids=[0])
    return r.results[0]["out"]
```
